# Optimizing a Trainium2 kernel written in Bass

```python
import jax, jax.numpy as jnp
from jax import lax
import numpy as np

D_MODEL = 1024
BATCH = 1
SEQ = 1024
DEPTH = 1

N_MEM = 256
ATTN_HEADS = 8
ATTN_KV_HEADS = 2
ATTN_HEAD_DIM = 64
ATTN_WIDTH = ATTN_HEADS * ATTN_HEAD_DIM
ATTN_KV_WIDTH = ATTN_KV_HEADS * ATTN_HEAD_DIM
WINDOW = 128
BLOCK = 128
RET_HEADS = 4
RET_HEAD_DIM = 128
RET_WIDTH = RET_HEADS * RET_HEAD_DIM
RET_CHUNK = 128
MIX_WIDTH = ATTN_WIDTH + RET_WIDTH
IN_COLS = ATTN_WIDTH + 2 * ATTN_KV_WIDTH + 4 * RET_WIDTH
XA_HEADS = 4
XA_HEAD_DIM = D_MODEL // XA_HEADS
D_FF = -(-(8 * D_MODEL) // (3 * 256)) * 256
ROPE_THETA = 10000.0
EPS = 1e-6

kernel_name = "hybrid_swa_retention_memxattn_block"

def rms_norm(x, w):
    xf = x.astype(jnp.float32)
    y = xf * lax.rsqrt(jnp.mean(xf * xf, axis=-1, keepdims=True) + EPS)
    return (y * w.astype(jnp.float32)).astype(x.dtype)

def rope(x):
    S, d = x.shape[1], x.shape[-1]
    inv_freq = ROPE_THETA ** (-jnp.arange(0, d, 2, dtype=jnp.float32) / d)
    ang = jnp.arange(S, dtype=jnp.float32)[:, None] * inv_freq[None, :]
    cos = jnp.cos(ang)[None, :, None, :]
    sin = jnp.sin(ang)[None, :, None, :]
    xf = x.astype(jnp.float32)
    x1, x2 = xf[..., : d // 2], xf[..., d // 2:]
    return jnp.concatenate([x1 * cos - x2 * sin, x1 * sin + x2 * cos], axis=-1).astype(x.dtype)

def window_attention(q, k, v, sink):
    B, S = q.shape[0], q.shape[1]
    nb = S // BLOCK
    G = ATTN_HEADS // ATTN_KV_HEADS
    qb = q.reshape(B, nb, BLOCK, ATTN_KV_HEADS, G, ATTN_HEAD_DIM)
    pad = ((0, 0), (BLOCK, BLOCK), (0, 0), (0, 0))
    kp = jnp.pad(k, pad).reshape(B, nb + 2, BLOCK, ATTN_KV_HEADS, ATTN_HEAD_DIM)
    vp = jnp.pad(v, pad).reshape(B, nb + 2, BLOCK, ATTN_KV_HEADS, ATTN_HEAD_DIM)
    kw = jnp.concatenate([kp[:, :-2], kp[:, 1:-1], kp[:, 2:]], axis=2)
    vw = jnp.concatenate([vp[:, :-2], vp[:, 1:-1], vp[:, 2:]], axis=2)
    s = jnp.einsum('bnqhgd,bnkhd->bhgnqk', qb, kw).astype(jnp.float32) * (ATTN_HEAD_DIM ** -0.5)
    blk = jnp.arange(nb)[:, None, None]
    qpos = blk * BLOCK + jnp.arange(BLOCK)[None, :, None]
    kpos = (blk - 1) * BLOCK + jnp.arange(3 * BLOCK)[None, None, :]
    valid = (jnp.abs(qpos - kpos) <= WINDOW) & (kpos >= 0) & (kpos < S)
    s = jnp.where(valid, s, -jnp.inf)
    sk = sink.astype(jnp.float32).reshape(ATTN_KV_HEADS, G)[None, :, :, None, None, None]
    m = jnp.maximum(jnp.max(s, axis=-1, keepdims=True), sk)
    p = jnp.exp(s - m)
    p = p / (jnp.sum(p, axis=-1, keepdims=True) + jnp.exp(sk - m))
    o = jnp.einsum('bhgnqk,bnkhd->bnqhgd', p.astype(v.dtype), vw)
    return o.reshape(B, S, ATTN_WIDTH)

def retention_scan(q, k, v, log_gamma, strict):
    C = q.shape[3]
    idx = jnp.arange(C, dtype=jnp.float32)
    diff = idx[:, None] - idx[None, :]
    mask = (diff > 0) if strict else (diff >= 0)
    lg = log_gamma[:, None, None]
    dmask = jnp.where(mask[None], jnp.exp(jnp.where(mask[None], diff[None], 0.0) * lg), 0.0)
    s = jnp.einsum('bhncd,bhnmd->bhncm', q, k) * dmask[None, :, None].astype(q.dtype)
    intra = jnp.einsum('bhncm,bhnme->bhnce', s, v)
    k_dec = k * jnp.exp((C - 1 - idx)[None, :] * log_gamma[:, None])[None, :, None, :, None].astype(k.dtype)
    kv = jnp.einsum('bhncd,bhnce->nbhde', k_dec, v)
    chunk_decay = jnp.exp(C * log_gamma).astype(kv.dtype)[None, :, None, None]

    def step(state, kv_n):
        return state * chunk_decay + kv_n, state

    _, prev = lax.scan(step, jnp.zeros_like(kv[0]), kv)
    q_dec = q * jnp.exp((idx + 1)[None, :] * log_gamma[:, None])[None, :, None, :, None].astype(q.dtype)
    inter = jnp.einsum('bhncd,nbhde->bhnce', q_dec, prev)
    return intra + inter

def retention(q, k, v, g, decay_fwd, decay_bwd, gn_w):
    B, S = q.shape[0], q.shape[1]
    N = S // RET_CHUNK
    q = rope(q)
    k = rope(k) * (RET_HEAD_DIM ** -0.5)

    def chunk(t):
        return t.transpose(0, 2, 1, 3).reshape(B, RET_HEADS, N, RET_CHUNK, RET_HEAD_DIM)

    lg_f = jax.nn.log_sigmoid(decay_fwd.astype(jnp.float32))
    lg_b = jax.nn.log_sigmoid(decay_bwd.astype(jnp.float32))
    y_f = retention_scan(chunk(q), chunk(k), chunk(v), lg_f, False).reshape(B, RET_HEADS, S, RET_HEAD_DIM)
    y_b = retention_scan(chunk(q[:, ::-1]), chunk(k[:, ::-1]), chunk(v[:, ::-1]), lg_b, True)
    y_b = y_b.reshape(B, RET_HEADS, S, RET_HEAD_DIM)[:, :, ::-1]
    y = (y_f + y_b).transpose(0, 2, 1, 3).astype(jnp.float32)
    mu = jnp.mean(y, axis=-1, keepdims=True)
    var = jnp.mean(jnp.square(y - mu), axis=-1, keepdims=True)
    yn = ((y - mu) * lax.rsqrt(var + EPS)).reshape(B, S, RET_WIDTH) * gn_w.astype(jnp.float32)
    return (jax.nn.silu(g.astype(jnp.float32)) * yn).astype(g.dtype)

def setup_inputs(seed: int = 0) -> dict:
    key = jax.random.key(seed)
    ks = jax.random.split(key, 24)
    f32 = jnp.float32

    def w(k, shape, fan_in):
        return jax.random.normal(k, shape, f32) * (fan_in ** -0.5)

    def gain(k, n):
        return 1.0 + 0.05 * jax.random.normal(k, (DEPTH, n), f32)

    base = 1.0 - jnp.exp2(-5.0 - jnp.arange(RET_HEADS, dtype=f32))
    base_logit = jnp.log(base / (1.0 - base))
    return {
        "x": jax.random.normal(ks[0], (BATCH, SEQ, D_MODEL), f32),
        "mem": jax.random.normal(ks[1], (BATCH, N_MEM, D_MODEL), f32),
        "norm_mix_pre": gain(ks[2], D_MODEL),
        "norm_mix_post": gain(ks[3], D_MODEL),
        "w_in": w(ks[4], (DEPTH, D_MODEL, IN_COLS), D_MODEL),
        "attn_sink": 0.5 * jax.random.normal(ks[5], (DEPTH, ATTN_HEADS), f32),
        "attn_out_norm": gain(ks[6], ATTN_WIDTH),
        "ret_decay_fwd": base_logit[None] + 0.1 * jax.random.normal(ks[7], (DEPTH, RET_HEADS), f32),
        "ret_decay_bwd": base_logit[None] + 0.1 * jax.random.normal(ks[8], (DEPTH, RET_HEADS), f32),
        "ret_gn": gain(ks[9], RET_WIDTH),
        "w_out": w(ks[10], (DEPTH, MIX_WIDTH, D_MODEL), MIX_WIDTH),
        "norm_xa_pre": gain(ks[11], D_MODEL),
        "norm_xa_post": gain(ks[12], D_MODEL),
        "norm_mem": gain(ks[13], D_MODEL),
        "xa_wq": w(ks[14], (DEPTH, D_MODEL, D_MODEL), D_MODEL),
        "xa_wkv": w(ks[15], (DEPTH, D_MODEL, 2 * D_MODEL), D_MODEL),
        "xa_wo": w(ks[16], (DEPTH, D_MODEL, D_MODEL), D_MODEL),
        "norm_ffn_pre": gain(ks[17], D_MODEL),
        "norm_ffn_post": gain(ks[18], D_MODEL),
        "ffn_w_gu": w(ks[19], (DEPTH, D_MODEL, 2 * D_FF), D_MODEL),
        "ffn_w_down": w(ks[20], (DEPTH, D_FF, D_MODEL), D_FF),
    }

def reference(x, mem, norm_mix_pre, norm_mix_post, w_in, attn_sink, attn_out_norm,
              ret_decay_fwd, ret_decay_bwd, ret_gn, w_out, norm_xa_pre, norm_xa_post,
              norm_mem, xa_wq, xa_wkv, xa_wo, norm_ffn_pre, norm_ffn_post,
              ffn_w_gu, ffn_w_down):
    B, S, _ = x.shape
    M = mem.shape[1]
    o_k = ATTN_WIDTH
    o_v = o_k + ATTN_KV_WIDTH
    o_r = o_v + ATTN_KV_WIDTH
    for l in range(DEPTH):
        h = rms_norm(x, norm_mix_pre[l])
        z = h @ w_in[l]
        aq = z[..., :o_k].reshape(B, S, ATTN_HEADS, ATTN_HEAD_DIM)
        ak = z[..., o_k:o_v].reshape(B, S, ATTN_KV_HEADS, ATTN_HEAD_DIM)
        av = z[..., o_v:o_r].reshape(B, S, ATTN_KV_HEADS, ATTN_HEAD_DIM)
        rq, rk, rv, rg = jnp.split(z[..., o_r:], 4, axis=-1)
        a = window_attention(rope(aq), rope(ak), av, attn_sink[l])
        a = rms_norm(a, attn_out_norm[l])
        r = retention(rq.reshape(B, S, RET_HEADS, RET_HEAD_DIM),
                      rk.reshape(B, S, RET_HEADS, RET_HEAD_DIM),
                      rv.reshape(B, S, RET_HEADS, RET_HEAD_DIM),
                      rg, ret_decay_fwd[l], ret_decay_bwd[l], ret_gn[l])
        mix = jnp.concatenate([a, r], axis=-1) @ w_out[l]
        x = x + rms_norm(mix, norm_mix_post[l])

        h = rms_norm(x, norm_xa_pre[l])
        mn = rms_norm(mem, norm_mem[l])
        q = (h @ xa_wq[l]).reshape(B, S, XA_HEADS, XA_HEAD_DIM)
        kv = (mn @ xa_wkv[l]).reshape(B, M, 2, XA_HEADS, XA_HEAD_DIM)
        s = jnp.einsum('bshd,bmhd->bhsm', q, kv[:, :, 0]).astype(jnp.float32) * (XA_HEAD_DIM ** -0.5)
        p = jax.nn.softmax(s, axis=-1).astype(x.dtype)
        xo = jnp.einsum('bhsm,bmhd->bshd', p, kv[:, :, 1]).reshape(B, S, D_MODEL) @ xa_wo[l]
        x = x + rms_norm(xo, norm_xa_post[l])

        h = rms_norm(x, norm_ffn_pre[l])
        gate, up = jnp.split(h @ ffn_w_gu[l], 2, axis=-1)
        f = (jax.nn.silu(gate) * up) @ ffn_w_down[l]
        x = x + rms_norm(f, norm_ffn_post[l])
    return x


_drawn_inputs = setup_inputs


def setup_inputs(seed=0):
    import zlib

    import numpy as np

    out = dict(_drawn_inputs(seed))
    spreads = {}
    factors = {'attn_sink': 8.0, 'ret_gn': 2.868}
    for name, (base, spread) in spreads.items():
        noise = np.random.default_rng([zlib.crc32(name.encode()), seed]).standard_normal(out[name].shape)
        drawn = base * np.exp(spread * noise) if base else spread * noise
        out[name] = __import__('jax').numpy.asarray(drawn.astype(out[name].dtype))
    for name, factor in factors.items():
        out[name] = (out[name] * factor).astype(out[name].dtype)
    return out
```

```python
from contextlib import ExitStack

import concourse.bass as bass
from concourse import mybir
import numpy as np

F32 = mybir.dt.float32
F32R = mybir.dt.float32r
ALU = mybir.AluOpType
ACT = mybir.ActivationFunctionType
AX = mybir.AxisListType

P = 128
D = 1024
S = 1024
NT = S // P
NK = D // P
N_MEM = 256
NM = N_MEM // P
AH, AKV, AD = 8, 2, 64
G = AH // AKV
RH, RD = 4, 128
XH, XD = 4, 256
DFF = 2816
EPS = 1e-6
MASKED = -1e30

C_Q, C_K, C_V = 0, AH * AD, AH * AD + AKV * AD
C_RQ = C_V + AKV * AD
C_RK, C_RV, C_RG = C_RQ + RH * RD, C_RQ + 2 * RH * RD, C_RQ + 3 * RH * RD
IN_COLS = C_RG + RH * RD
ZP = 8
ZW = IN_COLS // ZP
A_SCALE = AD ** -0.5
R_SCALE = RD ** -0.5
X_SCALE = XD ** -0.5

RING = 4
FG = 256
NG = DFF // FG

U_Z = 0
U_O = U_Z + ZP * NK
U_KV = U_O + 2 * NK
U_Q = U_KV + 4 * NK
U_XO = U_Q + 2 * NK
U_F = U_XO + 2 * NK
U_END = U_F + NG * (NK + 4)

TURNED = dict(x=0, qk=16, c=42, mem=58, h2=62, k=78, h3=82)
ACT_EV = dict(x=0, z=16, qk=80, c=93, o=109, mem=125, h2=129, kv=145, k=153, q=157, xo=173, h3=189, end=205)
DVE_EV = dict(x=0, qk=16, c=29, mem=45, h2=49, h3=65, end=81)
TILES = dict(z=0, o=56, kv=70, q=74, xo=88, f=102)


ROPE_A = 9 * NT
ROPE_R = ROPE_A + 5 * NT
F_EV = DVE_EV["end"] + 4
I_H2, I_H3, I_END = 18, 34, 50
SEQ = [("post", 0)] + [step for t in range(1, NT) for step in (("post", t), ("pre", t - 1))] + [("pre", NT - 1)]


def turn_bank(n):
    if n < TURNED["mem"]:
        return (n - (TURNED["c"] if n >= TURNED["c"] else 0)) % 8
    return 4 + (n - (TURNED["h3"] if n >= TURNED["h3"] else TURNED["h2"] if n >= TURNED["h2"] else TURNED["mem"])) % 4


def kv_seen(c, t):
    return ACT_EV["h2"] + 6 * c + t + 1


def H2_HI(t):
    return ACT_EV["h2"] + 6 * (t // 2) + 2 + 2 * (t % 2)


def width(n):
    return (min(n + 2, NT) - max(n - 1, 0)) * P


def host_constants():
    def rope(d):
        inv = np.float32(10000.0) ** (-np.arange(0, d, 2, dtype=np.float32) / np.float32(d))
        ang = np.arange(S, dtype=np.float32)[:, None] * inv.astype(np.float32)[None, :]
        t = np.stack([np.cos(ang.astype(np.float64)), np.sin(ang.astype(np.float64))]).astype(np.float32)
        return t.reshape(2, NT, P, d // 2).transpose(2, 0, 1, 3).reshape(P, -1)

    i = np.arange(P, dtype=np.float32)
    diff = i[None, :] - i[:, None]
    off = (np.arange(3 * P)[None, :] - P) - np.arange(P)[:, None]
    band = np.where(np.abs(off) <= P, 0.0, MASKED).astype(np.float32)
    decay = np.concatenate([np.maximum(diff, 0), np.maximum(-diff, 0),
                            np.broadcast_to(np.concatenate([i + 1, P - i]), (P, 2 * P))], 1).astype(np.float32)
    jv = np.repeat(np.stack([P - 1 - i, i], 1), RH, axis=1).astype(np.float32)
    return {
        "rope_tables": np.ascontiguousarray(np.concatenate([rope(AD), rope(RD)], 1)),
        "band": np.ascontiguousarray(band),
        "decay_powers": np.ascontiguousarray(decay),
        "value_powers": np.ascontiguousarray(jv),
        "identity": np.eye(P, dtype=np.float32),
    }


def build(nc, x, mem, norm_mix_pre, norm_mix_post, w_in, attn_sink, attn_out_norm, ret_decay_fwd,
          ret_decay_bwd, ret_gn, w_out, norm_xa_pre, norm_xa_post, norm_mem, xa_wq, xa_wkv, xa_wo,
          norm_ffn_pre, norm_ffn_post, ffn_w_gu, ffn_w_down, rope_tables, band_mask, decay_powers,
          value_powers, identity, out):
    with ExitStack() as ctx:
        def sb(name, shape, dt=F32):
            return ctx.enter_context(nc.sbuf_tensor(name, shape, dt))

        def sem(name):
            return ctx.enter_context(nc.semaphore(name))

        def overlay(*layouts):
            made = {}
            for n, layout in enumerate(layouts):
                with ExitStack() as inner:
                    use = ctx if n == len(layouts) - 1 else inner
                    for name, shape, dt in layout:
                        made[name] = use.enter_context(nc.sbuf_tensor(name, shape, dt))
            return made

        ident = sb("ident", [P, P])
        band = sb("band", [P, 3 * P])
        raw = sb("raw", [P, RING, 512])
        w_hi = sb("w_hi", [P, RING, 512], F32R)
        w_lo = sb("w_lo", [P, RING, 512], F32R)
        gain_a = sb("gain_a", [P, D])
        gain_b = sb("gain_b", [P, D])
        dtab = sb("dtab", [P, RH, P])
        zero = sb("zero", [P, 1])
        eps = sb("eps", [P, 1])
        one = sb("one", [P, 1])
        sink = sb("sink", [P, AH])
        nsink = sb("nsink", [P, AH])
        dec = sb("dec", [P, 2 * RH])
        dec_t = sb("dec_t", [P, 3, 2 * RH])
        lg = sb("lg", [P, 2 * RH])
        cdec = sb("cdec", [P, 2 * RH])
        vpow = sb("vpow", [P, 2 * RH])
        vtab = sb("vtab", [P, 2 * RH])
        ss = sb("ss", [P, 64])
        rms = sb("rms", [P, 64])
        rstd = sb("rstd", [P, 64])
        wmx = sb("wmx", [P, NT, AH])
        wnm = sb("wnm", [P, NT, AH])
        wds = wmx
        wes = sb("wes", [P, NT, AH])
        wrs = sb("wrs", [P, NT, AH])
        wden = wrs
        wrd = sb("wrd", [P, NT, AH])
        st6 = sb("st6", [P, RH * NT, 6])
        mv = sb("mv", [P, RH * NT, 2])
        rsd = sb("rsd", [P, RH * NT])
        rrs = sb("rrs", [P, RH * NT])

        H = overlay(
            [("t_hi", [P, NK, S], F32R), ("t_lo", [P, NK, S], F32R)],
            [("states", [P, NT, 2, RD], F32), ("qdec", [P, 2, NT, P], F32), ("smt", [P, NT, P], F32)],
            [("qT", [P, G, S], F32), ("kT", [P, S], F32), ("rqT", [P, RH, S], F32), ("rkT", [P, RH, S], F32),
             ("sm", [P, 2, G, 3 * P], F32)],
        )
        t_hi, t_lo, qT, kT, rqT, rkT, sm = (H[n] for n in ("t_hi", "t_lo", "qT", "kT", "rqT", "rkT", "sm"))
        states, qdec, smt = H["states"], H["qdec"], H["smt"]
        vdec = sm[:, :, :, :].rearrange("p a b c -> p (a b c)")[:, 0:NT * 2 * RD].rearrange(
            "p (n f e) -> p n f e", n=NT, f=2)

        Z = overlay(
            [("z", [P, NT, IN_COLS], F32), ("ropet", [P, 2 * NT * (AD // 2 + RD // 2)], F32),
             ("rope_a", [P, D], F32), ("rope_b", [P, D], F32)],
            [("z_1", [P, NT, IN_COLS], F32), ("junk_c", [P, 1536], F32), ("qtab", [P, RH, 2, P], F32),
             ("pTw", [P, G, 3 * P], F32)],
            [("z_2", [P, NT, IN_COLS], F32), ("junk_d", [P, 1536], F32), ("qtab_1", [P, RH, 2, P], F32),
             ("powers", [P, 4 * P], F32)],
            [("x1_1", [P, NT, D], F32), ("y_1", [P, NT, D], F32), ("vM_1", [P, NM, D], F32), ("kM_1", [P, NK, N_MEM], F32),
             ("m_hi", [P, NK, N_MEM], F32R), ("m_lo", [P, NK, N_MEM], F32R), ("mem_t", [P, NM, D], F32)],
            [("x1_2", [P, NT, D], F32), ("y_2", [P, NT, D], F32), ("vM_2", [P, NM, D], F32), ("kM_2", [P, NK, N_MEM], F32),
             ("pTx", [P, NM, XH, 512], F32), ("px", [P, 2, XH, N_MEM], F32)],
            [("x1_3", [P, NT, D], F32), ("qX", [P, NK, S], F32)],
            [("x1_4", [P, NT, D], F32), ("y_4", [P, NT, D], F32), ("f_hi", [P, 2, 2, S], F32R),
             ("f_lo", [P, 2, 2, S], F32R), ("gs", [P, 4, 512], F32)],
            [("x1", [P, NT, D], F32), ("y", [P, NT, D], F32), ("vM", [P, NM, D], F32), ("kM", [P, NK, N_MEM], F32),
             ("free_1", [P, 4096], F32), ("junk", [P, D], F32), ("free_2", [P, D], F32)],
        )
        z, ropet, rope_a, rope_b, junk_c, qtab, pTw, powers = (
            Z[n] for n in ("z", "ropet", "rope_a", "rope_b", "junk_c", "qtab", "pTw", "powers"))
        m_hi, m_lo, mem_t, pTx, px, qX, f_hi, f_lo, gs, x1, y, vM, kM, junk = (
            Z[n] for n in ("m_hi", "m_lo", "mem_t", "pTx", "px", "qX", "f_hi", "f_lo", "gs", "x1", "y", "vM", "kM", "junk"))
        kst = mem_t

        na, nr = NT * AD // 2, NT * RD // 2
        rt = ropet[:, :]
        cos_a = rt[:, 0:na].rearrange("p (t d) -> p t d", t=NT)
        sin_a = rt[:, na:2 * na].rearrange("p (t d) -> p t d", t=NT)
        cos_r = rt[:, 2 * na:2 * na + nr].rearrange("p (t d) -> p t d", t=NT)
        sin_r = rt[:, 2 * na + nr:2 * na + 2 * nr].rearrange("p (t d) -> p t d", t=NT)

        ps = ctx.enter_context(nc.psum_tensor("ps", [P, 8, 512], F32))

        w_loaded = [sem(f"w_loaded{i}") for i in range(RING)]
        w_rounded = sem("w_rounded")
        w_split = sem("w_split")
        w_used = sem("w_used")
        tile_done = sem("tile_done")
        turned = sem("turned")
        act_ev = sem("act_ev")
        dve_ev = sem("dve_ev")
        x_in = [sem(f"x_in{t}") for t in range(NT)]
        c_in = sem("c_in")
        band_in = sem("band_in")
        rope_in = sem("rope_in")
        ga_in = sem("ga_in")
        gb_in = sem("gb_in")
        mem_in = sem("mem_in")
        pow_in = sem("pow_in")
        x1_in = [sem(f"x1_in{t}") for t in range(NT)]
        set_up = sem("set_up")
        summed = sem("summed")
        rooted = sem("rooted")
        inverted = sem("inverted")
        scaled = sem("scaled")
        added = sem("added")
        roped = sem("roped")
        gate_on = sem("gate_on")
        gated = sem("gated")
        dk_a = sem("dk_a")
        dk_v = sem("dk_v")
        sc_ready = sem("sc_ready")
        w_max = sem("w_max")
        w_small = sem("w_small")
        w_exp = sem("w_exp")
        w_tr = sem("w_tr")
        w_pa = sem("w_pa")
        w_pd = sem("w_pd")
        w_pv = sem("w_pv")
        w_den = sem("w_den")
        w_a = sem("w_a")
        r_vd = sem("r_vd")
        r_qd = sem("r_qd")
        r_st = sem("r_st")
        r_kv = sem("r_kv")
        r_sm = sem("r_sm")
        r_scan = sem("r_scan")
        r_y = sem("r_y")
        r_yc = sem("r_yc")
        r_bn = sem("r_bn")
        r_rt = sem("r_rt")
        r_post = sem("r_post")
        r_n = sem("r_n")
        x_sc = sem("x_sc")
        x_mx = sem("x_mx")
        x_exp = sem("x_exp")
        x_nrm = sem("x_nrm")
        x_tr = sem("x_tr")
        x_pa = sem("x_pa")
        x_pd = sem("x_pd")
        x_pv = sem("x_pv")
        x_hi = sem("x_hi")
        x_lo = sem("x_lo")
        f_silu = sem("f_silu")
        f_high = sem("f_high")
        f_low = sem("f_low")
        f_bank = sem("f_bank")
        y_zero = sem("y_zero")
        stored = sem("stored")

        win_v = w_in[0].rearrange("(k p) m -> k p m", p=P)
        wout_v = w_out[0].rearrange("(k p) m -> k p m", p=P)
        wkv_v = xa_wkv[0].rearrange("(k p) m -> k p m", p=P)
        wq_v = xa_wq[0].rearrange("(k p) m -> k p m", p=P)
        wo_v = xa_wo[0].rearrange("(k p) m -> k p m", p=P)
        wgu_v = ffn_w_gu[0].rearrange("(k p) (two f) -> k p two f", p=P, two=2)
        wd_v = ffn_w_down[0].rearrange("(k p) m -> k p m", p=P)
        x_v = x[0].rearrange("(t p) d -> t p d", p=P)
        out_v = out[0].rearrange("(t p) d -> t p d", p=P)

        def rows(v, lo=0, hi=None):
            return v[0:1, :].partition_broadcast(P) if hi is None else v[0:1, lo:hi].partition_broadcast(P)

        def bank(b, n=512):
            return ps[:, b, 0:n]

        def qk_dst(i):
            g, c = i // 2, slice(i % 2 * 512, (i % 2 + 1) * 512)
            if g < G:
                return qT[:, g, c]
            if g == G:
                return kT[:, c]
            g -= G + 1
            return rqT[:, g, c] if g < RH else rkT[:, g - RH, c]

        block = ctx.enter_context(nc.Block())

        @block.sync
        def _(sp):
            def load(u, k, dst, src, first=False):
                if not first:
                    sp.wait_ge(w_split, u + (k - RING + 1))
                sp.dma_start(dst, src).then_inc(w_loaded[k % RING], 16)

            def piece(u, view, cols, width, first=False):
                for k in range(NK):
                    load(u, k, raw[:, k % RING, 0:width], view[k, :, cols], first and k < RING)

            piece(U_Z, win_v, slice(0, ZW), ZW, True)
            with sp.Fori(1, ZP) as c:
                piece(c * NK + U_Z, win_v, bass.ds(c * ZW, ZW), ZW)
            with sp.Fori(0, 2) as c:
                piece(c * NK + U_O, wout_v, bass.ts(c, 512), 512)
            with sp.Fori(0, 4) as c:
                piece(c * NK + U_KV, wkv_v, bass.ts(c, 512), 512)
            with sp.Fori(0, 2) as c:
                piece(c * NK + U_Q, wq_v, bass.ts(c, 512), 512)
            with sp.Fori(0, 2) as c:
                piece(c * NK + U_XO, wo_v, bass.ts(c, 512), 512)

            def gate_up(u, g):
                for k in range(NK):
                    load(u, k, raw[:, k % RING, :].rearrange("p (two f) -> p two f", two=2),
                         wgu_v[k, :, :, bass.ds(g * FG, FG)])

            def down(u, g):
                for c in range(2):
                    for kk in range(2):
                        load(u, 2 * c + kk, raw[:, 2 * c + kk, :], wd_v[g * 2 + kk, :, c * 512:(c + 1) * 512])

            gate_up(U_F, 0)
            with sp.Fori(0, NG // 2) as i:
                u = i * 24 + (U_F + NK)
                gate_up(u, i * 2 + 1)
                down(u + 8, i * 2)
                gate_up(u + 12, i * 2 + 2)
                down(u + 20, i * 2 + 1)
            down(U_END - 4, NG - 1)
            for t in range(NT):
                sp.wait_ge(added, 2 * NT + t + 1)
                sp.dma_start(out_v[t], x1[:, t, :]).then_inc(stored, 16)
            sp.wait_ge(stored, 16 * NT)

        @block.gpsimd
        def _(pool):
            def split(u, u0, k, width, first=False, loads=None):
                s = k % RING
                n = 16 * ((u0 + k) // RING + 1)
                pool.wait_ge(w_loaded[s], n if loads is None else loads * 16 + n)
                if not first:
                    pool.wait_ge(w_used, u + (k - RING + 1))
                nc.gpsimd.tensor_tensor(w_hi[:, s, 0:width], raw[:, s, 0:width],
                                        zero[:, 0:1].broadcast_to([P, width]), ALU.add).then_inc(w_rounded, 1)
                pool.wait_ge(w_rounded, u + (k + 1))
                nc.gpsimd.tensor_tensor(w_lo[:, s, 0:width], raw[:, s, 0:width], w_hi[:, s, 0:width].bitcast(F32),
                                        ALU.subtract).then_inc(w_split, 1)

            pool.wait_ge(set_up, 1)
            for k in range(NK):
                split(U_Z, U_Z, k, ZW, k < RING)
            with pool.Fori(1, ZP) as c:
                for k in range(NK):
                    split(c * NK + U_Z, U_Z, k, ZW, loads=c * 2)
            pool.wait_ge(gb_in, 32)
            for t in range(NT):
                pool.wait_ge(gate_on, t + 1)
                g = z[:, t, C_RG:C_RG + RH * RD]
                nc.gpsimd.tensor_tensor(g, g, gain_b[:, 512:1024], ALU.mult).then_inc(gated, 1)
            pool.wait_ge(dk_v, 12)
            pool.wait_ge(sc_ready, NT * AH)
            for h in range(RH):
                if h:
                    pool.wait_ge(r_y, NT * h)
                for f in range(2):
                    nc.gpsimd.tensor_tensor(qdec[:, f, :, :], rqT[:, h, :].rearrange("p (n i) -> p n i", n=NT),
                                            qtab[:, h, f, :].unsqueeze(1).broadcast_to([P, NT, P]),
                                            ALU.mult).then_inc(r_qd, 1)
            for base, pieces in ((U_O, 2), (U_KV, 4), (U_Q, 2), (U_XO, 2)):
                with pool.Fori(0, pieces) as c:
                    for k in range(NK):
                        split(c * NK + base, base, k, 512, loads=c * 2)
            for k in range(NK):
                split(U_F, U_F, k, 512)
                if k == RING - 1:
                    pool.wait_ge(turned, TURNED["h3"] + 2 * NT)
                    for t in range(NT):
                        nc.gpsimd.memset(y[:, t, :], 0.0).then_inc(y_zero, 1)
            with pool.Fori(0, NG // 2) as i:
                for k in range(24):
                    split(i * 24 + (U_F + NK), U_F + NK, k, 512, loads=i * 6)
            for k in range(4):
                split(U_END - 4, U_END - 4, k, 512)

        @block.tensor
        def _(pe):
            def transpose_to(b, col, src):
                return nc.tensor.transpose(ps[:, b, col:col + P], src, ident[:, :])

            def three(out, a_hi, a_lo, b_hi, b_lo, start, stop):
                nc.tensor.matmul(out, a_hi, b_hi, start=start, stop=False)
                nc.tensor.matmul(out, a_hi, b_lo, start=False, stop=False)
                return nc.tensor.matmul(out, a_lo, b_hi, start=False, stop=stop)

            def product(u, nbanks, width, bank_free, operands, b0=0, nk=NK, done=tile_done):
                for k in range(nk):
                    pe.wait_ge(w_split, u + (k + 1))
                    for t in range(nbanks):
                        if k == 0:
                            bank_free(t)
                        last = three(ps[:, b0 + t, 0:width], *operands(k, t), k == 0, k == nk - 1)
                        if t == nbanks - 1:
                            last.then_inc(w_used, 1)
                        elif k == nk - 1:
                            last.then_inc(done, 1)

            def rows_by_weights(hi, lo, width):
                def operands(k, t):
                    s = k % RING
                    return (hi[:, k, t * P:(t + 1) * P], lo[:, k, t * P:(t + 1) * P],
                            w_hi[:, s, 0:width], w_lo[:, s, 0:width])
                return operands

            def turn_rows(t, srcs, b, ready, free):
                ready()
                for half in range(2):
                    free(half)
                    for j in range(4):
                        last = transpose_to(b + half, j * P, srcs(4 * half + j))
                    last.then_inc(turned, 1)

            pe.wait_ge(c_in, 16 * 5)
            for t in range(NT):
                turn_rows(t, lambda j: z[:, t, j * P:(j + 1) * P], 2 * (t % 4),
                          lambda: pe.wait_ge(scaled, t + 1),
                          lambda half: pe.wait_ge(dve_ev, 2 * (t - 4) + half + 1) if t >= 4 else None)
            pe.wait_ge(dve_ev, DVE_EV["qk"])
            with pe.Fori(0, ZP) as c:
                product(c * NK + U_Z, NT, ZW,
                        lambda t: pe.wait_ge(act_ev, c * NT + (ACT_EV["z"] - NT + t + 1)),
                        rows_by_weights(t_hi, t_lo, ZW))

            groups = [(lambda t, j=j: z[:, t, C_Q + j * P:C_Q + (j + 1) * P], ROPE_A)
                      for j in range(G)]
            groups += [(lambda t: z[:, t, C_K:C_V], ROPE_A)]
            groups += [(lambda t, o=C_RQ + h * RD: z[:, t, o:o + RD], ROPE_R) for h in range(2 * RH)]
            pe.wait_ge(act_ev, ACT_EV["qk"])
            for i in range(2 * len(groups)):
                src, steps = groups[i // 2]
                pe.wait_ge(roped, steps)
                if i >= 8:
                    if i % 2 == 0:
                        pe.wait_ge(act_ev, ACT_EV["qk"] + (i - 8) // 2 + 1)
                    else:
                        pe.wait_ge(dve_ev, DVE_EV["qk"] + (i - 8) // 2 + 1)
                for j in range(4):
                    last = transpose_to(i % 8, j * P, src(4 * (i % 2) + j))
                last.then_inc(turned, 1)

            pe.wait_ge(act_ev, ACT_EV["c"])
            pe.wait_ge(dve_ev, DVE_EV["c"])

            def keys(n):
                return max(n - 1, 0), min(n + 2, NT)

            def scores(s):
                n, g = divmod(s, AKV)
                k0, k1 = keys(n)
                for j in range(G):
                    if s:
                        pe.wait_ge(w_max, G * (s - 1) + j + 1)
                    nc.tensor.matmul(ps[:, j, 0:(k1 - k0) * P], qT[g * AD:(g + 1) * AD, j, n * P:(n + 1) * P],
                                     kT[g * AD:(g + 1) * AD, k0 * P:k1 * P], start=True, stop=True).then_inc(sc_ready, 1)

            def copied(q):
                s, j = divmod(q, G)
                pe.wait_ge(w_pd if j % 2 else w_pa, 2 * s + j // 2 + 1)

            def turn_probs(s, j):
                n, g = divmod(s, AKV)
                k0, k1 = keys(n)
                q = G * s + j
                pe.wait_ge(w_exp, 5 * s + j + 1)
                if q >= 3:
                    copied(q - 3)
                for kb in range(k1 - k0):
                    last = transpose_to(4 + q % 3, kb * P, sm[:, s % 2, j, kb * P:(kb + 1) * P])
                last.then_inc(w_tr, 1)

            def values(s, j):
                n, g = divmod(s, AKV)
                k0, k1 = keys(n)
                copied(G * s + j)
                if g == 0 and j == 0 and n:
                    pe.wait_ge(w_a, n)
                h = g * G + j
                for kb in range(k1 - k0):
                    last = nc.tensor.matmul(ps[:, 7, h * AD:(h + 1) * AD], pTw[:, j, kb * P:(kb + 1) * P],
                                            z[:, k0 + kb, C_V + g * AD:C_V + (g + 1) * AD],
                                            start=kb == 0, stop=kb == k1 - k0 - 1)
                last.then_inc(w_pv, 1)

            steps = NT * AKV
            scores(0)
            for s in range(steps):
                if s + 1 < steps:
                    scores(s + 1)
                for j in range(3):
                    turn_probs(s, j)
                values(s, 0)
                turn_probs(s, 3)
                for j in range(1, G):
                    values(s, j)

            def chunk_products(h):
                for n in range(NT):
                    if n % 4 == 0 and h:
                        pe.wait_ge(r_sm, 2 * (h - 1) + n // 4 + 1)
                    if n == 0 and h == 0:
                        pe.wait_ge(w_max, NT * AH)
                    last = nc.tensor.matmul(ps[:, n // 4, (n % 4) * P:(n % 4 + 1) * P], rkT[:, h, n * P:(n + 1) * P],
                                            rqT[:, h, n * P:(n + 1) * P], start=True, stop=True)
                    if n % 4 == 3:
                        last.then_inc(r_st, 1)
                pe.wait_ge(r_vd, 2 * h + 2)
                if h == 0:
                    pe.wait_ge(w_pa, 2 * steps)
                    pe.wait_ge(w_pd, 2 * steps)
                else:
                    pe.wait_ge(r_scan, 14 * h)
                for n in range(NT):
                    nc.tensor.matmul(ps[:, 2 + n // 2, (n % 2) * 256:(n % 2 + 1) * 256],
                                     z[:, n, C_RK + h * RD:C_RK + (h + 1) * RD], vdec[:, n, :, :],
                                     start=True, stop=True).then_inc(r_kv, 1)

            def outputs(h):
                pe.wait_ge(r_qd, 2 * h + 2)
                pe.wait_ge(r_scan, 14 * (h + 1))
                for n in range(NT):
                    if n % 4 == 0:
                        pe.wait_ge(r_sm, 2 * h + n // 4 + 1)
                        if h:
                            pe.wait_ge(r_yc, 2 * (h - 1) + n // 4 + 1)
                        elif n == 0:
                            pe.wait_ge(w_a, NT)
                    o = ps[:, 6 + n // 4, (n % 4) * P:(n % 4 + 1) * P]
                    terms = [(smt[:, n, :], z[:, n, C_RV + h * RD:C_RV + (h + 1) * RD])]
                    if n:
                        terms.append((qdec[:, 0, n, :], states[:, n, 0, :]))
                    if n < NT - 1:
                        terms.append((qdec[:, 1, n, :], states[:, n, 1, :]))
                    for i, (a, b) in enumerate(terms):
                        last = nc.tensor.matmul(o, a, b, start=i == 0, stop=i == len(terms) - 1)
                    last.then_inc(r_y, 1)

            chunk_products(0)
            for h in range(RH):
                if h + 1 < RH:
                    chunk_products(h + 1)
                outputs(h)

            for t in range(NT):
                turn_rows(t, lambda j: z[:, t, (C_Q if j < 4 else C_RQ) + (j % 4) * P:][:, 0:P], 2 * (t % 4),
                          lambda: pe.wait_ge(scaled, NT + t + 1),
                          lambda half: pe.wait_ge(dve_ev, DVE_EV["c"] + 2 * (t - 4) + half + 1) if t >= 4 else (
                              pe.wait_ge(r_yc, 2 * RH)))
            pe.wait_ge(dve_ev, DVE_EV["mem"])
            with pe.Fori(0, 2) as c:
                product(c * NK + U_O, NT, 512,
                        lambda t: pe.wait_ge(act_ev, c * NT + (ACT_EV["o"] - NT + t + 1)),
                        rows_by_weights(t_hi, t_lo, 512))

            def turn_tile(stage, n0, t):
                turn_rows(t, lambda j: y[:, t, j * P:(j + 1) * P], 4 + 2 * (t % 2),
                          lambda: pe.wait_ge(scaled, n0 + t + 1),
                          lambda half: pe.wait_ge(dve_ev, DVE_EV[stage] + 2 * (t - 2) + half + 1) if t >= 2 else None)

            pe.wait_ge(act_ev, ACT_EV["mem"])
            for t in range(NM):
                turn_rows(t, lambda j: mem_t[:, t, j * P:(j + 1) * P], 4 + 2 * t,
                          lambda: pe.wait_ge(scaled, 2 * NT + t + 1), lambda half: None)
            pe.wait_ge(dve_ev, DVE_EV["h2"])
            for c in range(4):
                product(c * NK + U_KV, NM, 512, lambda t: pe.wait_ge(act_ev, kv_seen(c - 2, t)) if c >= 2 else None,
                        rows_by_weights(m_hi, m_lo, 512), b0=2 * (c % 2))
                turn_tile("h2", 2 * NT + NM, 2 * c)
                turn_tile("h2", 2 * NT + NM, 2 * c + 1)
            pe.wait_ge(act_ev, kv_seen(3, 1))
            for i in range(4):
                for j in range(4):
                    kt, mt = divmod(4 * i + j, NM)
                    last = transpose_to(i, j * P, kst[:, mt, kt * P:(kt + 1) * P])
                last.then_inc(turned, 1)

            pe.wait_ge(dve_ev, DVE_EV["h3"])
            pe.wait_ge(act_ev, ACT_EV["q"])

            def features_by_rows(k, t):
                s, m, half = k % RING, t // 2, t % 2
                return (w_hi[:, s, m * P:(m + 1) * P], w_lo[:, s, m * P:(m + 1) * P],
                        t_hi[:, k, half * 512:(half + 1) * 512], t_lo[:, k, half * 512:(half + 1) * 512])

            with pe.Fori(0, 2) as c:
                product(c * NK + U_Q, NT, 512,
                        lambda t: pe.wait_ge(act_ev, c * NT + (ACT_EV["q"] - NT + t + 1)),
                        features_by_rows)

            pe.wait_ge(act_ev, ACT_EV["xo"])

            def mem_scores(t):
                if t >= 2:
                    pe.wait_ge(x_exp, XH * (t - 1))
                for h in range(XH):
                    o = ps[:, 2 * (t % 2) + h // 2, (h % 2) * N_MEM:(h % 2 + 1) * N_MEM]
                    for kk in range(2):
                        last = nc.tensor.matmul(o, qX[:, 2 * h + kk, t * P:(t + 1) * P], kM[:, 2 * h + kk, :],
                                                start=kk == 0, stop=kk == 1)
                last.then_inc(x_sc, 1)

            def mem_turn(t):
                pe.wait_ge(x_nrm, 2 * t + 2)
                for b in range(2):
                    if t:
                        pe.wait_ge(x_pd if b else x_pa, t)
                    for j in range(4):
                        h, mm = 2 * b + j // 2, j % 2
                        last = transpose_to(4 + b, j * P, px[:, t % 2, h, mm * P:(mm + 1) * P])
                    last.then_inc(x_tr, 1)

            def mem_values(half):
                pe.wait_ge(x_pa, 4 * (half + 1))
                pe.wait_ge(x_pd, 4 * (half + 1))
                for d in range(NK):
                    n = NK * half + d
                    if n >= 2:
                        pe.wait_ge(x_lo, n - 1)
                    for mm in range(NM):
                        last = nc.tensor.matmul(ps[:, 6 + d % 2, :], vM[:, mm, d * P:(d + 1) * P], pTx[:, mm, d // 2, :],
                                                start=mm == 0, stop=mm == NM - 1)
                    last.then_inc(x_pv, 1)

            mem_scores(0)
            for t in range(NT):
                if t + 1 < NT:
                    mem_scores(t + 1)
                mem_turn(t)
                if t % 4 == 3:
                    mem_values(t // 4)

            pe.wait_ge(x_lo, 2 * NK)
            pe.wait_ge(x_exp, XH * NT)
            with pe.Fori(0, 2) as c:
                product(c * NK + U_XO, NT, 512,
                        lambda t: pe.wait_ge(act_ev, c * NT + (ACT_EV["xo"] - NT + t + 1)),
                        rows_by_weights(t_hi, t_lo, 512))
            pe.wait_ge(act_ev, ACT_EV["h3"])
            for t in range(NT):
                turn_tile("h3", 3 * NT + NM, t)

            pe.wait_ge(dve_ev, DVE_EV["end"])

            def gate_up(u, seen=None):
                def operands(k, t):
                    s, ch, half, up = k % RING, t // 4, t // 2 % 2, t % 2
                    w = slice(up * FG + ch * P, up * FG + (ch + 1) * P)
                    return (w_hi[:, s, w], w_lo[:, s, w],
                            t_hi[:, k, half * 512:(half + 1) * 512], t_lo[:, k, half * 512:(half + 1) * 512])
                product(u, 8, 512, lambda t: None if seen is None else pe.wait_ge(dve_ev, seen + (t + 1)), operands)

            def down(u, buf, low, free):
                pe.wait_ge(f_low, low)
                for c in range(2):
                    def operands(k, t):
                        s = 2 * c + k
                        return (f_hi[:, buf, k, t * P:(t + 1) * P], f_lo[:, buf, k, t * P:(t + 1) * P],
                                w_hi[:, s, :], w_lo[:, s, :])
                    product(u + 2 * c, NT, 512, lambda t: pe.wait_ge(dve_ev, free(c, t)), operands, nk=2, done=f_bank)

            gate_up(U_F)
            pe.wait_ge(dve_ev, F_EV)
            with pe.Fori(0, NG // 2) as i:
                for odd in range(2):
                    u = i * 24 + (U_F + NK + 12 * odd)
                    start = i * 40 + (F_EV + 20 * odd)
                    gate_up(u, start - 8)
                    down(u + NK, odd, i * 8 + 4 * (odd + 1),
                         lambda c, t: start + ((t // 2 + 1) if c == 0 else (4 + t + 1)))
            last_start = F_EV + 20 * (NG - 1)
            down(U_END - 4, (NG - 1) % 2, 4 * NG, lambda c, t: last_start + 8 * (c - 1) + t + 1)

        @block.scalar
        def _(act):
            def square_root(i, src, scratch, n, ready):
                ready()
                nc.scalar.activation(scratch, src, ACT.Square, accum_out=ss[:, i:i + 1]).then_inc(summed, 1)
                act.wait_ge(summed, i + 1)
                nc.scalar.activation(rms[:, i:i + 1], ss[:, i:i + 1], ACT.Sqrt, bias=eps[:, 0:1],
                                     scale=1.0 / n).then_inc(rooted, 1)

            def hi_parts(n, dst, col):
                for half in range(2):
                    act.wait_ge(turned, n + half + 1)
                    b = turn_bank(n + half)
                    nc.scalar.activation(dst[:, 4 * half:4 * half + 4, col:col + P],
                                         bank(b).rearrange("p (k i) -> p k i", k=4), ACT.Copy).then_inc(act_ev, 1)

            def tile_ready(stage, c, t, nbanks, u):
                if t < nbanks - 1:
                    act.wait_ge(tile_done, c * (nbanks - 1) + (TILES[stage] + t + 1))
                else:
                    act.wait_ge(w_used, u + NK)

            for t in range(NT):
                act.dma_start(z[:, t, 0:D], x_v[t]).then_inc(x_in[t], 16)
                if t == 0:
                    act.dma_start(gain_a[:, :], rows(norm_mix_pre)).then_inc(ga_in, 16)
                    act.dma_start(ident[:, :], identity).then_inc(c_in, 16)
            act.dma_start(sink[:, :], rows(attn_sink)).then_inc(c_in, 16)
            act.dma_start(dec[:, 0:RH], rows(ret_decay_fwd)).then_inc(c_in, 16)
            act.dma_start(dec[:, RH:2 * RH], rows(ret_decay_bwd)).then_inc(c_in, 16)
            act.dma_start(vpow[:, :], value_powers).then_inc(c_in, 16)
            act.dma_start(ropet[:, :], rope_tables).then_inc(rope_in, 16)
            act.dma_start(band[:, :], band_mask).then_inc(band_in, 16)
            act.dma_start(gain_b[:, 0:512], rows(attn_out_norm)).then_inc(gb_in, 16)
            act.dma_start(gain_b[:, 512:1024], rows(ret_gn)).then_inc(gb_in, 16)

            act.wait_ge(set_up, 3)
            for t in range(NT):
                square_root(t, z[:, t, 0:D], z[:, t, D:2 * D], D, lambda: act.wait_ge(x_in[t], 16))
                if t:
                    hi_parts(TURNED["x"] + 2 * (t - 1), t_hi, (t - 1) * P)
            hi_parts(TURNED["x"] + 2 * (NT - 1), t_hi, (NT - 1) * P)

            with act.Fori(0, ZP) as c:
                for t in range(NT):
                    tile_ready("z", c, t, NT, c * NK + U_Z)
                    nc.scalar.activation(z[:, t, bass.ds(c * ZW, ZW)], bank(t, ZW), ACT.Copy).then_inc(act_ev, 1)
            act.wait_ge(scaled, NT)
            act.dma_start(gain_a[:, :], rows(norm_mix_post)).then_inc(ga_in, 16)
            act.wait_ge(act_ev, ACT_EV["qk"])
            for t in range(NT):
                g = z[:, t, C_RG:C_RG + RH * RD]
                nc.scalar.activation(g, g, ACT.Silu).then_inc(gate_on, 1)
            act.wait_ge(roped, ROPE_R)
            act.dma_start(powers[:, :], decay_powers).then_inc(pow_in, 16)
            for i in range(0, 26, 2):
                act.wait_ge(turned, TURNED["qk"] + i + 1)
                nc.scalar.activation(qk_dst(i), bank(i % 8), ACT.Copy).then_inc(act_ev, 1)

            act.wait_ge(c_in, 16 * 5)
            nc.scalar.activation(dec_t[:, 0, :], dec[:, :], ACT.Abs).then_inc(dk_a, 1)
            act.wait_ge(dk_a, 1)
            nc.scalar.activation(dec_t[:, 1, :], dec_t[:, 0, :], ACT.Exp, scale=-1.0).then_inc(dk_a, 1)
            act.wait_ge(dk_a, 2)
            nc.scalar.activation(dec_t[:, 2, :], dec_t[:, 1, :], ACT.Ln, bias=one[:, 0:1]).then_inc(dk_a, 1)
            act.wait_ge(dk_v, 9)
            nc.scalar.activation(dtab[:, :, :], dtab[:, :, :], ACT.Exp).then_inc(dk_a, 1)
            act.wait_ge(dk_v, 10)
            nc.scalar.activation(vtab[:, :], vtab[:, :], ACT.Exp).then_inc(dk_a, 1)
            nc.scalar.activation(cdec[:, :], lg[:, :], ACT.Exp, scale=float(P)).then_inc(dk_a, 1)
            act.wait_ge(pow_in, 16)
            for h in range(RH):
                for f in range(2):
                    nc.scalar.activation(qtab[:, h, f, :], powers[:, (2 + f) * P:(3 + f) * P], ACT.Exp,
                                         scale=lg[:, f * RH + h:f * RH + h + 1]).then_inc(dk_a, 1)

            def exponentials(s, heads):
                n, g = divmod(s, AKV)
                nk = width(n)
                for j in heads:
                    act.wait_ge(w_small, 2 * s + 1)
                    h = g * G + j
                    p = sm[:, s % 2, j, 0:nk]
                    nc.scalar.activation(p, p, ACT.Exp, bias=wnm[:, n, h:h + 1], scale=A_SCALE,
                                         accum_out=wrs[:, n, h:h + 1]).then_inc(w_exp, 1)

            def sink_term(s):
                n, g = divmod(s, AKV)
                act.wait_ge(w_small, 2 * s + 2)
                nc.scalar.activation(wes[:, n, g * G:(g + 1) * G], wds[:, n, g * G:(g + 1) * G],
                                     ACT.Exp).then_inc(w_exp, 1)

            def copy_probs(s, j):
                q = G * s + j
                act.wait_ge(w_tr, q + 1)
                if s:
                    act.wait_ge(w_pv, q - G + 1)
                nk = width(s // AKV)
                nc.scalar.activation(pTw[:, j, 0:nk], bank(4 + q % 3, nk), ACT.Copy).then_inc(w_pa, 1)

            steps = NT * AKV
            act.wait_ge(dk_v, 12)
            exponentials(0, range(G))
            sink_term(0)
            for s in range(steps):
                more = s + 1 < steps
                copy_probs(s, 0)
                if more:
                    exponentials(s + 1, (0, 1))
                copy_probs(s, 2)
                if more:
                    exponentials(s + 1, (2, 3))
                    sink_term(s + 1)

            def decayed_values(h):
                act.wait_ge(r_kv, NT * h) if h else act.wait_ge(w_tr, G * steps)
                for f in range(2):
                    nc.scalar.activation(vdec[:, :, f, :], z[:, :, C_RV + h * RD:C_RV + (h + 1) * RD], ACT.Copy,
                                         scale=vtab[:, f * RH + h:f * RH + h + 1]).then_inc(r_vd, 1)

            decayed_values(0)
            for h in range(RH):
                if h + 1 < RH:
                    decayed_values(h + 1)
                for b in range(2):
                    act.wait_ge(r_y, NT * h + 4 * (b + 1))
                    nc.scalar.activation(z[:, 4 * b:4 * b + 4, C_RQ + h * RD:C_RQ + (h + 1) * RD],
                                         bank(6 + b).rearrange("p (n e) -> p n e", n=4), ACT.Copy).then_inc(r_yc, 1)
            act.wait_ge(r_qd, 2 * RH)
            act.dma_start(mem_t[:, :, :], mem[0].rearrange("(m p) d -> p m d", p=P)).then_inc(mem_in, 16)
            act.wait_ge(r_bn, 2 * RH * NT)
            nc.scalar.activation(rsd[:, :], mv[:, :, 1], ACT.Sqrt, bias=eps[:, 0:1]).then_inc(r_rt, 1)
            for t in range(NT):
                square_root(NT + t, z[:, t, 0:512], junk_c[:, 0:512], 512, lambda: act.wait_ge(w_a, t + 1))
            for t in range(NT):
                hi_parts(TURNED["c"] + 2 * t, t_hi, t * P)

            act.wait_ge(scaled, 2 * NT)
            act.wait_ge(turned, TURNED["mem"])
            act.dma_start(gain_b[:, :], rows(norm_mem)).then_inc(gb_in, 16)
            for t in range(NT):
                act.dma_start(x1[:, t, :], x_v[t]).then_inc(x1_in[t], 16)
            for m in range(NM):
                square_root(2 * NT + m, mem_t[:, m, :], kM[:, 0:4, :].rearrange("p a b -> p (a b)"), D,
                            lambda: act.wait_ge(mem_in, 16))
            act.wait_ge(scaled, 2 * NT + NM)
            act.dma_start(gain_b[:, :], rows(norm_xa_pre)).then_inc(gb_in, 16)

            def product_out(stage, u0, dst):
                with act.Fori(0, 2) as c:
                    for t in range(NT):
                        tile_ready(stage, c, t, NT, c * NK + u0)
                        nc.scalar.activation(dst(c, t), bank(t), ACT.Copy).then_inc(act_ev, 1)

            product_out("o", U_O, lambda c, t: y[:, t, bass.ts(c, 512)])
            for m in range(NM):
                hi_parts(TURNED["mem"] + 2 * m, m_hi, m * P)

            def sums(seq, i0, items, scratch, added0):
                for i in items:
                    kind, t = seq[i]
                    if kind == "post":
                        square_root(i0 + i, y[:, t, :], scratch, D, lambda: None)
                    else:
                        square_root(i0 + i, x1[:, t, :], scratch, D, lambda: act.wait_ge(added, added0 + t + 1))

            scratch = kM[:, 0:4, :].rearrange("p a b -> p (a b)")
            act.wait_ge(act_ev, ACT_EV["h2"])
            done = 0

            def until(t, i0, scr, added0):
                nonlocal done
                end = SEQ.index(("pre", min(t, NT - 1))) + 1
                sums(SEQ, i0, range(done, end), scr, added0)
                done = max(done, end)

            until(1, I_H2, scratch, 0)
            for c in range(4):
                for t in range(NM):
                    if t == 0:
                        act.wait_ge(tile_done, TILES["kv"] + c + 1)
                    else:
                        act.wait_ge(w_used, U_KV + NK * (c + 1))
                    dst = kst if c < 2 else vM
                    nc.scalar.activation(dst[:, t, (c % 2) * 512:(c % 2 + 1) * 512], bank(2 * (c % 2) + t),
                                         ACT.Copy).then_inc(act_ev, 1)
                for t in (2 * c, 2 * c + 1):
                    hi_parts(TURNED["h2"] + 2 * t, t_hi, t * P)
                    until(t + 2, I_H2, scratch, 0)
            for i in range(4):
                act.wait_ge(turned, TURNED["k"] + i + 1)
                nc.scalar.activation(kM[:, 2 * i:2 * i + 2, :], bank(i).rearrange("p (k m) -> p k m", k=2),
                                     ACT.Copy).then_inc(act_ev, 1)
            act.wait_ge(added, NT)
            act.dma_start(gain_a[:, :], rows(norm_xa_post)).then_inc(ga_in, 16)
            act.wait_ge(scaled, 3 * NT + NM)
            act.dma_start(gain_b[:, :], rows(norm_ffn_pre)).then_inc(gb_in, 16)

            product_out("q", U_Q, lambda c, t: qX[:, bass.ds(c * 4 + t // 2, 1), (t % 2) * 512:(t % 2 + 1) * 512])

            def mem_exp(t):
                act.wait_ge(x_mx, 2 * t + 2)
                if t >= 2:
                    act.wait_ge(x_tr, 2 * (t - 1))
                for h in range(XH):
                    nc.scalar.activation(px[:, t % 2, h, :], ps[:, 2 * (t % 2) + h // 2, (h % 2) * N_MEM:(h % 2 + 1) * N_MEM],
                                         ACT.Exp, bias=wnm[:, t, h:h + 1], scale=X_SCALE,
                                         accum_out=wrs[:, t, h:h + 1]).then_inc(x_exp, 1)

            mem_exp(0)
            for t in range(NT):
                if t + 1 < NT:
                    mem_exp(t + 1)
                act.wait_ge(x_tr, 2 * t + 1)
                if t >= 4:
                    act.wait_ge(x_pv, NK)
                nc.scalar.activation(pTx[:, :, 0:2, (t % 4) * P:(t % 4 + 1) * P],
                                     bank(4).rearrange("p (h m i) -> p m h i", h=2, m=2), ACT.Copy).then_inc(x_pa, 1)
                if t % 4 == 3:
                    half = t // 4
                    for d in range(NK):
                        act.wait_ge(x_pv, NK * half + d + 1)
                        nc.scalar.activation(t_hi[:, d, half * 512:(half + 1) * 512], bank(6 + d % 2),
                                             ACT.Copy).then_inc(x_hi, 1)

            product_out("xo", U_XO, lambda c, t: y[:, t, bass.ts(c, 512)])
            act.wait_ge(act_ev, ACT_EV["h3"])
            done = 0
            until(1, I_H3, junk[:, :], NT)
            for t in range(NT):
                hi_parts(TURNED["h3"] + 2 * t, t_hi, t * P)
                until(t + 2, I_H3, junk[:, :], NT)
            act.wait_ge(added, 2 * NT)
            act.dma_start(gain_a[:, :], rows(norm_ffn_post)).then_inc(ga_in, 16)

            def group(g, seen, first=False):
                def silu(p):
                    act.wait_ge(tile_done, g * 7 + (TILES["f"] + 2 * p + 1))
                    if not first:
                        act.wait_ge(f_low, g * 4 + (p - 3))
                    nc.scalar.activation(gs[:, p, :], bank(2 * p), ACT.Silu).then_inc(f_silu, 1)

                def high(p):
                    act.wait_ge(dve_ev, seen + (p + 1))
                    nc.scalar.activation(f_hi[:, buf, p // 2, (p % 2) * 512:(p % 2 + 1) * 512], gs[:, p, :],
                                         ACT.Copy).then_inc(f_high, 1)
                silu(0)
                silu(1)
                high(0)
                silu(2)
                high(1)
                silu(3)
                high(2)
                high(3)

            buf = 0
            group(0, DVE_EV["end"], True)
            with act.Fori(0, NG // 2) as i:
                for buf in (1, 0):
                    group(i * 2 + (2 - buf), i * 40 + (F_EV + 20 * (1 - buf)))
            for t in range(NT):
                square_root(I_END + t, y[:, t, :], junk[:, :], D,
                            lambda: act.wait_ge(dve_ev, F_EV + 20 * (NG - 1) + NT + t + 1))

        @block.vector
        def _(dve):
            def invert(i):
                dve.wait_ge(rooted, i + 1)
                nc.vector.reciprocal(rstd[:, i:i + 1], rms[:, i:i + 1]).then_inc(inverted, 1)
                dve.wait_ge(inverted, i + 1)

            def lo_parts(hi_count, n, hi, lo, col):
                for half in range(2):
                    dve.wait_ge(act_ev, hi_count + half + 1)
                    b = turn_bank(n + half)
                    nc.vector.tensor_tensor(lo[:, 4 * half:4 * half + 4, col:col + P],
                                            bank(b).rearrange("p (k i) -> p k i", k=4),
                                            hi[:, 4 * half:4 * half + 4, col:col + P].bitcast(F32),
                                            ALU.subtract).then_inc(dve_ev, 1)

            nc.vector.memset(zero[:, :], 0.0).then_inc(set_up, 1)
            nc.vector.memset(eps[:, :], EPS).then_inc(set_up, 1)
            nc.vector.memset(one[:, :], 1.0).then_inc(set_up, 1)

            dve.wait_ge(ga_in, 16)
            for t in range(NT):
                invert(t)
                nc.vector.scalar_tensor_tensor(out=z[:, t, 0:D], in0=z[:, t, 0:D], scalar=rstd[:, t:t + 1],
                                               in1=gain_a[:, :], op0=ALU.mult, op1=ALU.mult).then_inc(scaled, 1)
                if t:
                    lo_parts(ACT_EV["x"] + 2 * (t - 1), TURNED["x"] + 2 * (t - 1), t_hi, t_lo, (t - 1) * P)
            lo_parts(ACT_EV["x"] + 2 * (NT - 1), TURNED["x"] + 2 * (NT - 1), t_hi, t_lo, (NT - 1) * P)

            dve.wait_ge(rope_in, 16)
            n = 0
            for c0, c1, d, cos, sin, pieces in ((C_Q, C_V, AD, cos_a, sin_a, 2), (C_RQ, C_RV, RD, cos_r, sin_r, 6)):
                heads = (c1 - c0) // d
                a = rope_a[:, 0:c1 - c0].rearrange("p (h two d) -> p h two d", h=heads, two=2)
                b = rope_b[:, 0:c1 - c0].rearrange("p (h two d) -> p h two d", h=heads, two=2)
                for t in range(NT):
                    dve.wait_ge(act_ev, ACT_EV["z"] + NT * (pieces - 1) + t + 1)
                    if n:
                        dve.wait_ge(roped, n)
                    v = z[:, t, c0:c1].rearrange("p (h two d) -> p h two d", h=heads, two=2)
                    cb = cos[:, t, :].unsqueeze(1).broadcast_to([P, 2 * heads, d // 2])
                    sb_ = sin[:, t, :].unsqueeze(1).broadcast_to([P, heads, d // 2])
                    nc.vector.tensor_tensor(a.rearrange("p h two d -> p (h two) d"),
                                            v.rearrange("p h two d -> p (h two) d"), cb, ALU.mult).then_inc(roped, 1)
                    nc.vector.tensor_tensor(b[:, :, 0, :], v[:, :, 1, :], sb_, ALU.mult).then_inc(roped, 1)
                    nc.vector.tensor_tensor(b[:, :, 1, :], v[:, :, 0, :], sb_, ALU.mult).then_inc(roped, 1)
                    dve.wait_ge(roped, n + 3)
                    outs = [(0, heads, v)]
                    if d == AD:
                        q = z[:, t, C_Q:C_K].rearrange("p (j g two d) -> p g j two d", g=AKV, j=G, two=2)
                        outs = [(g * G, (g + 1) * G, q[:, g, :, :, :]) for g in range(AKV)] + [(AH, heads, v[:, AH:heads, :, :])]
                    for h0, h1, o in outs:
                        nc.vector.tensor_tensor(o[:, :, 0, :], a[:, h0:h1, 0, :], b[:, h0:h1, 0, :],
                                                ALU.subtract).then_inc(roped, 1)
                        nc.vector.tensor_tensor(o[:, :, 1, :], a[:, h0:h1, 1, :], b[:, h0:h1, 1, :],
                                                ALU.add).then_inc(roped, 1)
                    n += 3 + 2 * len(outs)
            for i in range(1, 26, 2):
                dve.wait_ge(turned, TURNED["qk"] + i + 1)
                nc.vector.tensor_copy(qk_dst(i), bank(i % 8)).then_inc(dve_ev, 1)

            dve.wait_ge(c_in, 16 * 5)
            nc.vector.tensor_scalar(nsink[:, :], sink[:, :], -1.0, None, ALU.mult).then_inc(w_den, 1)
            dve.wait_ge(dk_a, 3)
            nc.vector.scalar_tensor_tensor(out=lg[:, :], in0=dec[:, :], scalar=0.0, in1=dec_t[:, 2, :],
                                           op0=ALU.min, op1=ALU.subtract).then_inc(dk_v, 1)
            dve.wait_ge(pow_in, 16)
            dve.wait_ge(dk_v, 1)
            for h in range(RH):
                nc.vector.tensor_scalar(dtab[:, h, :], powers[:, P:2 * P], lg[:, RH + h:RH + h + 1], None,
                                        ALU.mult).then_inc(dk_v, 1)
                dve.wait_ge(dk_v, 2 + 2 * h)
                nc.vector.scalar_tensor_tensor(out=dtab[:, h, :], in0=powers[:, 0:P], scalar=lg[:, h:h + 1],
                                               in1=dtab[:, h, :], op0=ALU.mult, op1=ALU.add).then_inc(dk_v, 1)
            nc.vector.tensor_tensor(vtab[:, :], vpow[:, :], lg[:, :], ALU.mult).then_inc(dk_v, 1)
            dve.wait_ge(dk_a, 4)
            nc.vector.tensor_scalar(dtab[:, :, :], dtab[:, :, :], R_SCALE, None, ALU.mult).then_inc(dk_v, 1)
            dve.wait_ge(dk_a, 14)
            nc.vector.tensor_scalar(qtab[:, :, :, :], qtab[:, :, :, :], R_SCALE, None, ALU.mult).then_inc(dk_v, 1)

            def maxima(s):
                n, g = divmod(s, AKV)
                nk = width(n)
                off = P if n == 0 else 0
                for j in range(G):
                    q = G * s + j
                    h = g * G + j
                    dve.wait_ge(sc_ready, q + 1)
                    if s >= 2:
                        dve.wait_ge(w_tr, G * (s - 2) + j + 1)
                    nc.vector.tensor_tensor_reduce(sm[:, s % 2, j, 0:nk], bank(j, nk), band[:, off:off + nk],
                                                   1.0, -3.0e38, ALU.add, ALU.max, wmx[:, n, h:h + 1]).then_inc(w_max, 1)
                dve.wait_ge(w_max, G * (s + 1))
                hs = slice(g * G, (g + 1) * G)
                nc.vector.scalar_tensor_tensor(out=wnm[:, n, hs], in0=wmx[:, n, hs], scalar=-A_SCALE, in1=nsink[:, hs],
                                               op0=ALU.mult, op1=ALU.min).then_inc(w_small, 1)
                dve.wait_ge(w_small, 2 * s + 1)
                nc.vector.tensor_tensor(wds[:, n, hs], sink[:, hs], wnm[:, n, hs], ALU.add).then_inc(w_small, 1)

            def copy_probs(s, j):
                q = G * s + j
                dve.wait_ge(w_tr, q + 1)
                if s:
                    dve.wait_ge(w_pv, q - G + 1)
                nk = width(s // AKV)
                nc.vector.tensor_copy(pTw[:, j, 0:nk], bank(4 + q % 3, nk)).then_inc(w_pd, 1)

            steps = NT * AKV
            dve.wait_ge(band_in, 16)
            dve.wait_ge(w_den, 1)
            maxima(0)
            for s in range(steps):
                if s + 1 < steps:
                    maxima(s + 1)
                copy_probs(s, 1)
                copy_probs(s, 3)
                if s % AKV == AKV - 1:
                    n = s // AKV
                    dve.wait_ge(w_exp, 5 * (s + 1))
                    nc.vector.tensor_tensor(wden[:, n, :], wrs[:, n, :], wes[:, n, :], ALU.add).then_inc(w_den, 1)
                    dve.wait_ge(w_den, 2 * n + 2)
                    nc.vector.reciprocal(wrd[:, n, :], wden[:, n, :]).then_inc(w_den, 1)
                    dve.wait_ge(w_den, 2 * n + 3)
                    dve.wait_ge(w_pv, G * (s + 1))
                    nc.vector.tensor_tensor(z[:, n, C_Q:C_K].rearrange("p (h d) -> p h d", h=AH),
                                            bank(7).rearrange("p (h d) -> p h d", h=AH),
                                            wrd[:, n, :].unsqueeze(2).broadcast_to([P, AH, AD]), ALU.mult).then_inc(w_a, 1)

            def decay_scores(h):
                for b in range(2):
                    dve.wait_ge(r_st, 2 * h + b + 1)
                    if h:
                        dve.wait_ge(r_y, NT * h)
                    nc.vector.tensor_tensor(smt[:, 4 * b:4 * b + 4, :], bank(b).rearrange("p (n i) -> p n i", n=4),
                                            dtab[:, h, :].unsqueeze(1).broadcast_to([P, 4, P]), ALU.mult).then_inc(r_sm, 1)

            def recurrences(h):
                k = 14 * h
                for i in range(NT - 1):
                    for f, n in ((0, i), (1, NT - 1 - i)):
                        dst = states[:, n + 1 if f == 0 else n - 1, f, :]
                        prod = ps[:, 2 + n // 2, (n % 2) * 256 + f * RD:(n % 2) * 256 + (f + 1) * RD]
                        dve.wait_ge(r_kv, NT * h + n // 2 * 2 + 2)
                        if i == 0:
                            nc.vector.tensor_copy(dst, prod).then_inc(r_scan, 1)
                        else:
                            dve.wait_ge(r_scan, k - 1)
                            nc.vector.scalar_tensor_tensor(out=dst, in0=states[:, n, f, :],
                                                           scalar=cdec[:, f * RH + h:f * RH + h + 1], in1=prod,
                                                           op0=ALU.mult, op1=ALU.add).then_inc(r_scan, 1)
                        k += 1

            def statistics(h):
                k = 2 * NT * h
                for n in range(NT):
                    dve.wait_ge(r_yc, 2 * h + n // 4 + 1)
                    nc.vector.bn_stats(st6[:, h * NT + n, :], z[:, n, C_RQ + h * RD:C_RQ + (h + 1) * RD]).then_inc(r_bn, 1)
                for n in range(NT):
                    dve.wait_ge(r_bn, k + n + 1)
                    nc.vector.bn_aggr(mv[:, h * NT + n, :], st6[:, h * NT + n, :]).then_inc(r_bn, 1)

            dve.wait_ge(dk_v, 12)
            for h in range(RH):
                decay_scores(h)
                recurrences(h)
                if h:
                    statistics(h - 1)
            statistics(RH - 1)
            dve.wait_ge(r_rt, 1)
            nc.vector.reciprocal(rrs[:, :], rsd[:, :]).then_inc(r_n, 1)
            dve.wait_ge(r_n, 1)
            dve.wait_ge(gb_in, 32)
            k = 1
            for t in range(NT):
                for h in range(RH):
                    v = z[:, t, C_RQ + h * RD:C_RQ + (h + 1) * RD]
                    i = h * NT + t
                    nc.vector.tensor_scalar(v, v, mv[:, i, 0:1], rrs[:, i:i + 1], ALU.subtract, ALU.mult).then_inc(r_n, 1)
                k += RH
                invert(NT + t)
                a = z[:, t, 0:512]
                nc.vector.scalar_tensor_tensor(out=a, in0=a, scalar=rstd[:, NT + t:NT + t + 1], in1=gain_b[:, 0:512],
                                               op0=ALU.mult, op1=ALU.mult).then_inc(r_n, 1)
                k += 1
                dve.wait_ge(r_n, k)
                dve.wait_ge(gated, t + 1)
                v = z[:, t, C_RQ:C_RQ + RH * RD]
                nc.vector.tensor_tensor(v, v, z[:, t, C_RG:C_RG + RH * RD], ALU.mult).then_inc(scaled, 1)
                if t:
                    lo_parts(ACT_EV["c"] + 2 * (t - 1), TURNED["c"] + 2 * (t - 1), t_hi, t_lo, (t - 1) * P)
            lo_parts(ACT_EV["c"] + 2 * (NT - 1), TURNED["c"] + 2 * (NT - 1), t_hi, t_lo, (NT - 1) * P)

            dve.wait_ge(gb_in, 48)
            for m in range(NM):
                invert(2 * NT + m)
                nc.vector.scalar_tensor_tensor(out=mem_t[:, m, :], in0=mem_t[:, m, :],
                                               scalar=rstd[:, 2 * NT + m:2 * NT + m + 1], in1=gain_b[:, :],
                                               op0=ALU.mult, op1=ALU.mult).then_inc(scaled, 1)
            for m in range(NM):
                lo_parts(ACT_EV["mem"] + 2 * m, TURNED["mem"] + 2 * m, m_hi, m_lo, m * P)

            def norm_steps(i0, items, added0, fresh):
                for i in items:
                    kind, t = SEQ[i]
                    invert(i0 + i)
                    r = rstd[:, i0 + i:i0 + i + 1]
                    if kind == "post":
                        after_product(t, r, added0, fresh)
                    else:
                        nc.vector.scalar_tensor_tensor(out=y[:, t, :], in0=x1[:, t, :], scalar=r, in1=gain_b[:, :],
                                                       op0=ALU.mult, op1=ALU.mult).then_inc(scaled, 1)

            posts = 0

            def after_product(t, r, added0, fresh):
                nonlocal posts
                posts += 1
                nc.vector.scalar_tensor_tensor(out=y[:, t, :], in0=y[:, t, :], scalar=r, in1=gain_a[:, :],
                                               op0=ALU.mult, op1=ALU.mult).then_inc(r_post, 1)
                dve.wait_ge(r_post, posts)
                if fresh:
                    dve.wait_ge(x1_in[t], 16)
                nc.vector.tensor_tensor(x1[:, t, :], x1[:, t, :], y[:, t, :], ALU.add).then_inc(added, 1)

            def norm_stage(i0, stage, added0, fresh):
                done = 0
                for t in range(-1, NT):
                    if t >= 0:
                        base = H2_HI(t) if stage == "h2" else ACT_EV["h3"] + 2 * t
                        lo_parts(base, TURNED[stage] + 2 * t, t_hi, t_lo, t * P)
                    end = SEQ.index(("pre", min(t + 2, NT - 1))) + 1
                    norm_steps(i0, range(done, end), added0, fresh)
                    done = max(done, end)

            dve.wait_ge(ga_in, 32)
            dve.wait_ge(gb_in, 64)
            norm_stage(I_H2, "h2", 0, True)

            def mem_max(t):
                dve.wait_ge(x_sc, t + 1)
                b = 2 * (t % 2)
                nc.vector.tensor_reduce(wmx[:, t, 0:XH],
                                        ps[:, b:b + 2, :].rearrange("p b (h m) -> p (b h) m", h=2), AX.X,
                                        ALU.max).then_inc(x_mx, 1)
                dve.wait_ge(x_mx, 2 * t + 1)
                nc.vector.tensor_scalar(wnm[:, t, 0:XH], wmx[:, t, 0:XH], -X_SCALE, None, ALU.mult).then_inc(x_mx, 1)

            mem_max(0)
            for t in range(NT):
                if t + 1 < NT:
                    mem_max(t + 1)
                dve.wait_ge(x_exp, XH * (t + 1))
                nc.vector.reciprocal(wrd[:, t, 0:XH], wrs[:, t, 0:XH]).then_inc(x_nrm, 1)
                dve.wait_ge(x_nrm, 2 * t + 1)
                nc.vector.tensor_tensor(px[:, t % 2, :, :], px[:, t % 2, :, :],
                                        wrd[:, t, 0:XH].unsqueeze(2).broadcast_to([P, XH, N_MEM]),
                                        ALU.mult).then_inc(x_nrm, 1)
                dve.wait_ge(x_tr, 2 * t + 2)
                if t >= 4:
                    dve.wait_ge(x_pv, NK)
                nc.vector.tensor_copy(pTx[:, :, 2:4, (t % 4) * P:(t % 4 + 1) * P],
                                      bank(5).rearrange("p (h m i) -> p m h i", h=2, m=2)).then_inc(x_pd, 1)
                if t % 4 == 3:
                    half = t // 4
                    for d in range(NK):
                        dve.wait_ge(x_hi, NK * half + d + 1)
                        c = slice(half * 512, (half + 1) * 512)
                        nc.vector.tensor_tensor(t_lo[:, d, c], bank(6 + d % 2), t_hi[:, d, c].bitcast(F32),
                                                ALU.subtract).then_inc(x_lo, 1)

            dve.wait_ge(ga_in, 48)
            dve.wait_ge(gb_in, 80)
            norm_stage(I_H3, "h3", NT, False)

            def group(g, u):
                def prod(p):
                    dve.wait_ge(f_silu, g * 4 + (p + 1))
                    if p < 3:
                        dve.wait_ge(tile_done, g * 7 + (TILES["f"] + 2 * p + 2))
                    else:
                        dve.wait_ge(w_used, u + NK)
                    nc.vector.tensor_tensor(gs[:, p, :], gs[:, p, :], bank(2 * p + 1), ALU.mult).then_inc(dve_ev, 1)

                def low(p):
                    dve.wait_ge(f_high, g * 4 + (p + 1))
                    c = slice((p % 2) * 512, (p % 2 + 1) * 512)
                    nc.vector.tensor_tensor(f_lo[:, buf, p // 2, c], gs[:, p, :], f_hi[:, buf, p // 2, c].bitcast(F32),
                                            ALU.subtract).then_inc(f_low, 1)
                prod(0)
                prod(1)
                low(0)
                prod(2)
                low(1)
                prod(3)
                low(2)
                low(3)

            def accumulate(d, u, before):
                for c in range(2):
                    for t in range(NT):
                        if t < NT - 1:
                            dve.wait_ge(f_bank, d * 14 + (7 * c + t + 1))
                        else:
                            dve.wait_ge(w_used, u + (2 * c + 2))
                        if c == 0 and t == 0:
                            dve.wait_ge(dve_ev, before)
                        v = y[:, t, c * 512:(c + 1) * 512]
                        nc.vector.tensor_tensor(v, bank(t), v, ALU.add).then_inc(dve_ev, 1)

            buf = 0
            dve.wait_ge(y_zero, NT)
            group(0, U_F)
            with dve.Fori(0, NG // 2) as i:
                for odd in range(2):
                    buf = 1 - odd
                    u = i * 24 + (U_F + NK + 12 * odd)
                    group(i * 2 + (1 + odd), u)
                    accumulate(i * 2 + odd, u + NK, i * 40 + (F_EV + 20 * odd))
            accumulate(NG - 1, U_END - 4, F_EV + 20 * (NG - 1))
            dve.wait_ge(ga_in, 64)
            dve.wait_ge(dve_ev, F_EV + 20 * (NG - 1) + 2 * NT)
            for t in range(NT):
                invert(I_END + t)
                after_product(t, rstd[:, I_END + t:I_END + t + 1], 0, False)


_INS = ["x", "mem", "norm_mix_pre", "norm_mix_post", "w_in", "attn_sink", "attn_out_norm", "ret_decay_fwd",
        "ret_decay_bwd", "ret_gn", "w_out", "norm_xa_pre", "norm_xa_post", "norm_mem", "xa_wq", "xa_wkv", "xa_wo",
        "norm_ffn_pre", "norm_ffn_post", "ffn_w_gu", "ffn_w_down"]
_OUTS = [((1, S, D), "float32")]


def kernel(**inputs):
    import numpy as _np
    import concourse.bacc as _bacc
    from concourse import mybir as _mybir
    from concourse.bass_utils import run_bass_kernel_spmd as _run

    nc = _bacc.Bacc("TRN2", target_bir_lowering=False, num_devices=1)
    arrays, args = {}, []
    for name in _INS:
        arrays[f"in_{name}_dram"] = _np.ascontiguousarray(inputs[name])
    for name, a in host_constants().items():
        arrays[f"const_{name}_dram"] = a
    for name, a in arrays.items():
        args.append(nc.dram_tensor(name, a.shape, _mybir.dt.from_np(a.dtype), kind="ExternalInput").ap())
    for i, (shape, dtype) in enumerate(_OUTS):
        dt = _mybir.dt.from_np(_np.dtype(dtype))
        args.append(nc.dram_tensor(f"out_{i}_dram", shape, dt, kind="ExternalOutput").ap())
    build(nc, *args)
    r = _run(nc, [arrays], core_ids=[0])
    return r.results[0]["out_0_dram"]
```

```python
from contextlib import ExitStack

import concourse.bass as bass
from concourse import mybir
import numpy as np

F32 = mybir.dt.float32
F32R = mybir.dt.float32r
ALU = mybir.AluOpType
ACT = mybir.ActivationFunctionType
AX = mybir.AxisListType

P = 128
D = 1024
S = 1024
NT = S // P
NK = D // P
N_MEM = 256
NM = N_MEM // P
AH, AKV, AD = 8, 2, 64
G = AH // AKV
RH, RD = 4, 128
XH, XD = 4, 256
DFF = 2816
EPS = 1e-6
MASKED = -1e30

C_Q, C_K, C_V = 0, AH * AD, AH * AD + AKV * AD
C_RQ = C_V + AKV * AD
C_RK, C_RV, C_RG = C_RQ + RH * RD, C_RQ + 2 * RH * RD, C_RQ + 3 * RH * RD
IN_COLS = C_RG + RH * RD
ZP = 8
ZW = IN_COLS // ZP
A_SCALE = AD ** -0.5
R_SCALE = RD ** -0.5
X_SCALE = XD ** -0.5

RING = 4
FG = 256
NG = DFF // FG

U_Z = 0
U_O = U_Z + ZP * NK
U_KV = U_O + 2 * NK
U_Q = U_KV + 4 * NK
U_XO = U_Q + 2 * NK
U_F = U_XO + 2 * NK
U_END = U_F + NG * (NK + 4)

TURNED = dict(x=0, qk=16, c=42, mem=58, h2=62, k=78, h3=82)
ACT_EV = dict(x=0, z=16, qk=80, c=93, o=109, mem=125, h2=129, kv=145, k=153, q=157, xo=173, h3=189, end=205)
DVE_EV = dict(x=0, qk=16, c=29, mem=45, h2=49, h3=65, end=81)
TILES = dict(z=0, o=56, kv=70, q=74, xo=88, f=102)


ROPE_A = 9 * NT
ROPE_R = ROPE_A + 5 * NT
F_EV = DVE_EV["end"] + 4
I_H2, I_H3, I_END = 18, 34, 50
SEQ = [("post", 0)] + [step for t in range(1, NT) for step in (("post", t), ("pre", t - 1))] + [("pre", NT - 1)]


def turn_bank(n):
    if n < TURNED["mem"]:
        return (n - (TURNED["c"] if n >= TURNED["c"] else 0)) % 8
    return 4 + (n - (TURNED["h3"] if n >= TURNED["h3"] else TURNED["h2"] if n >= TURNED["h2"] else TURNED["mem"])) % 4


def kv_seen(c, t):
    return ACT_EV["h2"] + 6 * c + t + 1


def H2_HI(t):
    return ACT_EV["h2"] + 6 * (t // 2) + 2 + 2 * (t % 2)


def width(n):
    return (min(n + 2, NT) - max(n - 1, 0)) * P


def host_constants():
    def rope(d):
        inv = np.float32(10000.0) ** (-np.arange(0, d, 2, dtype=np.float32) / np.float32(d))
        ang = np.arange(S, dtype=np.float32)[:, None] * inv.astype(np.float32)[None, :]
        t = np.stack([np.cos(ang.astype(np.float64)), np.sin(ang.astype(np.float64))]).astype(np.float32)
        return t.reshape(2, NT, P, d // 2).transpose(2, 0, 1, 3).reshape(P, -1)

    i = np.arange(P, dtype=np.float32)
    diff = i[None, :] - i[:, None]
    off = (np.arange(3 * P)[None, :] - P) - np.arange(P)[:, None]
    band = np.where(np.abs(off) <= P, 0.0, MASKED).astype(np.float32)
    decay = np.concatenate([np.maximum(diff, 0), np.maximum(-diff, 0),
                            np.broadcast_to(np.concatenate([i + 1, P - i]), (P, 2 * P))], 1).astype(np.float32)
    jv = np.repeat(np.stack([P - 1 - i, i], 1), RH, axis=1).astype(np.float32)
    return {
        "rope_tables": np.ascontiguousarray(np.concatenate([rope(AD), rope(RD)], 1)),
        "band": np.ascontiguousarray(band),
        "decay_powers": np.ascontiguousarray(decay),
        "value_powers": np.ascontiguousarray(jv),
        "identity": np.eye(P, dtype=np.float32),
    }


def build(nc, x, mem, norm_mix_pre, norm_mix_post, w_in, attn_sink, attn_out_norm, ret_decay_fwd,
          ret_decay_bwd, ret_gn, w_out, norm_xa_pre, norm_xa_post, norm_mem, xa_wq, xa_wkv, xa_wo,
          norm_ffn_pre, norm_ffn_post, ffn_w_gu, ffn_w_down, rope_tables, band_mask, decay_powers,
          value_powers, identity, out):
    with ExitStack() as ctx:
        def sb(name, shape, dt=F32):
            return ctx.enter_context(nc.sbuf_tensor(name, shape, dt))

        def sem(name):
            return ctx.enter_context(nc.semaphore(name))

        def overlay(*layouts):
            made = {}
            for n, layout in enumerate(layouts):
                with ExitStack() as inner:
                    use = ctx if n == len(layouts) - 1 else inner
                    for name, shape, dt in layout:
                        made[name] = use.enter_context(nc.sbuf_tensor(name, shape, dt))
            return made

        ident = sb("ident", [P, P])
        tables = sb("tables", [P, RH * P + 3 * P + RH * NT * 6])
        dtab = tables[:, 0:RH * P].rearrange("p (h i) -> p h i", h=RH)
        band = tables[:, RH * P:(RH + 3) * P]
        st6 = tables[:, (RH + 3) * P:].rearrange("p (n c) -> p n c", c=6)
        squares = tables[:, 0:D]
        raw = sb("raw", [P, RING, 512])
        w_hi = sb("w_hi", [P, RING, 512], F32R)
        w_lo = sb("w_lo", [P, RING, 512], F32R)
        gain_a = sb("gain_a", [P, D])
        gain_b = sb("gain_b", [P, D])
        zero = sb("zero", [P, 1])
        eps = sb("eps", [P, 1])
        one = sb("one", [P, 1])
        sink = sb("sink", [P, AH])
        nsink = sb("nsink", [P, AH])
        dec = sb("dec", [P, 2 * RH])
        dec_t = sb("dec_t", [P, 3, 2 * RH])
        lg = sb("lg", [P, 2 * RH])
        cdec = sb("cdec", [P, 2 * RH])
        vpow = sb("vpow", [P, 2 * RH])
        vtab = sb("vtab", [P, 2 * RH])
        ss = sb("ss", [P, 64])
        rms = sb("rms", [P, 64])
        rstd = sb("rstd", [P, 64])
        wmx = sb("wmx", [P, NT, AH])
        wnm = sb("wnm", [P, NT, AH])
        wds = wmx
        wes = sb("wes", [P, NT, AH])
        wrs = sb("wrs", [P, NT, AH])
        wden = wrs
        wrd = sb("wrd", [P, NT, AH])
        mv = sb("mv", [P, RH * NT, 2])
        rsd = sb("rsd", [P, RH * NT])
        rrs = sb("rrs", [P, RH * NT])

        H = overlay(
            [("t_hi", [P, NK, S], F32R), ("t_lo", [P, NK, S], F32R)],
            [("states", [P, 2, NT, 2, RD], F32), ("smt_even", [P, NT, P], F32)],
            [("qT", [P, G, S], F32), ("kT", [P, S], F32), ("rqT", [P, RH, S], F32), ("rkT", [P, RH, S], F32),
             ("sm", [P, 2, G, 3 * P], F32)],
        )
        t_hi, t_lo, qT, kT, rqT, rkT, sm = (H[n] for n in ("t_hi", "t_lo", "qT", "kT", "rqT", "rkT", "sm"))
        states = H["states"]
        qdec = [rkT, rqT]
        vdec = sm[:, :, :, :].rearrange("p a b c -> p (a b c)")[:, 0:NT * 2 * RD].rearrange(
            "p (n f e) -> p n f e", n=NT, f=2)
        smt = [H["smt_even"][:, :, :],
               sm[:, :, :, :].rearrange("p a b c -> p (a b c)")[:, NT * 2 * RD:NT * 2 * RD + NT * P].rearrange(
                   "p (n i) -> p n i", n=NT)]

        Z = overlay(
            [("z", [P, NT, IN_COLS], F32), ("ropet", [P, 2 * NT * (AD // 2 + RD // 2)], F32),
             ("rope_a", [P, D], F32), ("rope_b", [P, D], F32)],
            [("z_1", [P, NT, IN_COLS], F32), ("junk_c", [P, 1536], F32), ("qtab", [P, RH, 2, P], F32),
             ("pTw", [P, G, 3 * P], F32)],
            [("z_2", [P, NT, IN_COLS], F32), ("junk_d", [P, 1536], F32), ("qtab_1", [P, RH, 2, P], F32),
             ("powers", [P, 4 * P], F32)],
            [("x1_1", [P, NT, D], F32), ("y_1", [P, NT, D], F32), ("vM_1", [P, NM, D], F32), ("kM_1", [P, NK, N_MEM], F32),
             ("m_hi", [P, NK, N_MEM], F32R), ("m_lo", [P, NK, N_MEM], F32R), ("mem_t", [P, NM, D], F32)],
            [("x1_2", [P, NT, D], F32), ("y_2", [P, NT, D], F32), ("vM_2", [P, NM, D], F32), ("kM_2", [P, NK, N_MEM], F32),
             ("pTx", [P, NM, XH, 512], F32), ("px", [P, 2, XH, N_MEM], F32)],
            [("x1_3", [P, NT, D], F32), ("qX", [P, NK, S], F32)],
            [("x1_5", [P, NT, D], F32), ("y_5", [P, NT, D], F32), ("w_hi2", [P, RING, 512], F32R),
             ("w_lo2", [P, RING, 512], F32R)],
            [("x1_4", [P, NT, D], F32), ("y_4", [P, NT, D], F32), ("f_hi", [P, 2, 2, S], F32R),
             ("f_lo", [P, 2, 2, S], F32R), ("gs", [P, 4, 512], F32)],
            [("x1", [P, NT, D], F32), ("y", [P, NT, D], F32), ("vM", [P, NM, D], F32), ("kM", [P, NK, N_MEM], F32),
             ("free_1", [P, 4096], F32), ("free_2", [P, 2 * D], F32)],
        )
        z, ropet, rope_a, rope_b, junk_c, qtab, pTw, powers = (
            Z[n] for n in ("z", "ropet", "rope_a", "rope_b", "junk_c", "qtab", "pTw", "powers"))
        m_hi, m_lo, mem_t, pTx, px, qX, f_hi, f_lo, gs, x1, y, vM, kM = (
            Z[n] for n in ("m_hi", "m_lo", "mem_t", "pTx", "px", "qX", "f_hi", "f_lo", "gs", "x1", "y", "vM", "kM"))
        w_hi2, w_lo2 = Z["w_hi2"], Z["w_lo2"]
        kst = mem_t

        na, nr = NT * AD // 2, NT * RD // 2
        rt = ropet[:, :]
        cos_a = rt[:, 0:na].rearrange("p (t d) -> p t d", t=NT)
        sin_a = rt[:, na:2 * na].rearrange("p (t d) -> p t d", t=NT)
        cos_r = rt[:, 2 * na:2 * na + nr].rearrange("p (t d) -> p t d", t=NT)
        sin_r = rt[:, 2 * na + nr:2 * na + 2 * nr].rearrange("p (t d) -> p t d", t=NT)

        ps = ctx.enter_context(nc.psum_tensor("ps", [P, 8, 512], F32))

        w_loaded = [sem(f"w_loaded{i}") for i in range(RING)]
        w_rounded = sem("w_rounded")
        mem_rounded = sem("mem_rounded")
        w_split = sem("w_split")
        w_used = sem("w_used")
        tile_done = sem("tile_done")
        turned = sem("turned")
        act_ev = sem("act_ev")
        dve_ev = sem("dve_ev")
        x_in = [sem(f"x_in{t}") for t in range(NT)]
        ident_in = sem("ident_in")
        c_in = sem("c_in")
        band_in = sem("band_in")
        rope_in = sem("rope_in")
        ga_in = sem("ga_in")
        gb_in = sem("gb_in")
        mem_in = sem("mem_in")
        pow_in = sem("pow_in")
        x1_in = [sem(f"x1_in{t}") for t in range(NT)]
        set_up = sem("set_up")
        summed = sem("summed")
        rooted = sem("rooted")
        inverted = sem("inverted")
        scaled = sem("scaled")
        added = sem("added")
        roped = sem("roped")
        gate_on = sem("gate_on")
        gated = sem("gated")
        dk_a = sem("dk_a")
        dk_v = sem("dk_v")
        sc_ready = sem("sc_ready")
        w_max = sem("w_max")
        w_small = sem("w_small")
        w_exp = sem("w_exp")
        w_tr = sem("w_tr")
        w_pa = sem("w_pa")
        w_pd = sem("w_pd")
        w_pv = sem("w_pv")
        w_den = sem("w_den")
        w_a = sem("w_a")
        r_vd = sem("r_vd")
        r_qd = sem("r_qd")
        r_st = sem("r_st")
        r_kv = sem("r_kv")
        r_sm = sem("r_sm")
        r_scan = sem("r_scan")
        r_y = sem("r_y")
        r_yc = sem("r_yc")
        r_bn = sem("r_bn")
        r_rt = sem("r_rt")
        r_post = sem("r_post")
        r_n = sem("r_n")
        a_n = sem("a_n")
        mixed = sem("mixed")
        x_sc = sem("x_sc")
        x_mx = sem("x_mx")
        x_exp = sem("x_exp")
        x_nrm = sem("x_nrm")
        x_tr = sem("x_tr")
        x_pa = sem("x_pa")
        x_pd = sem("x_pd")
        x_pv = sem("x_pv")
        x_hi = sem("x_hi")
        x_lo = sem("x_lo")
        f_silu = sem("f_silu")
        f_high = sem("f_high")
        f_low = sem("f_low")
        f_bank = sem("f_bank")
        y_zero = sem("y_zero")
        stored = sem("stored")

        win_v = w_in[0].rearrange("(k p) m -> k p m", p=P)
        wout_v = w_out[0].rearrange("(k p) m -> k p m", p=P)
        wkv_v = xa_wkv[0].rearrange("(k p) m -> k p m", p=P)
        wq_v = xa_wq[0].rearrange("(k p) m -> k p m", p=P)
        wo_v = xa_wo[0].rearrange("(k p) m -> k p m", p=P)
        wgu_v = ffn_w_gu[0].rearrange("(k p) (two f) -> k p two f", p=P, two=2)
        wd_v = ffn_w_down[0].rearrange("(k p) m -> k p m", p=P)
        x_v = x[0].rearrange("(t p) d -> t p d", p=P)
        out_v = out[0].rearrange("(t p) d -> t p d", p=P)

        def rows(v, lo=0, hi=None):
            return v[0:1, :].partition_broadcast(P) if hi is None else v[0:1, lo:hi].partition_broadcast(P)

        def bank(b, n=512):
            return ps[:, b, 0:n]

        def qk_dst(i):
            g, c = i // 2, slice(i % 2 * 512, (i % 2 + 1) * 512)
            if g < G:
                return qT[:, g, c]
            if g == G:
                return kT[:, c]
            g -= G + 1
            return rqT[:, g, c] if g < RH else rkT[:, g - RH, c]

        block = ctx.enter_context(nc.Block())

        @block.sync
        def _(sp):
            def load(u, k, dst, src, first=False):
                if not first:
                    sp.wait_ge(w_split, u + (k - RING + 1))
                sp.dma_start(dst, src).then_inc(w_loaded[k % RING], 16)

            def piece(u, view, cols, width, first=False):
                for k in range(NK):
                    load(u, k, raw[:, k % RING, 0:width], view[k, :, cols], first and k < RING)
                    if first and k == RING - 1:
                        for t in range(1, NT):
                            sp.dma_start(z[:, t, 0:D], x_v[t]).then_inc(x_in[t], 16)

            sp.dma_start(z[:, 0, 0:D], x_v[0]).then_inc(x_in[0], 16)
            piece(U_Z, win_v, slice(0, ZW), ZW, True)
            with sp.Fori(1, ZP) as c:
                piece(c * NK + U_Z, win_v, bass.ds(c * ZW, ZW), ZW)
            with sp.Fori(0, 2) as c:
                piece(c * NK + U_O, wout_v, bass.ts(c, 512), 512)
            with sp.Fori(0, 4) as c:
                piece(c * NK + U_KV, wkv_v, bass.ts(c, 512), 512)
            with sp.Fori(0, 2) as c:
                piece(c * NK + U_Q, wq_v, bass.ts(c, 512), 512)
            with sp.Fori(0, 2) as c:
                piece(c * NK + U_XO, wo_v, bass.ts(c, 512), 512)

            def gate_up(u, g):
                for k in range(NK):
                    load(u, k, raw[:, k % RING, :].rearrange("p (two f) -> p two f", two=2),
                         wgu_v[k, :, :, bass.ds(g * FG, FG)])

            def down(u, g):
                for c in range(2):
                    for kk in range(2):
                        load(u, 2 * c + kk, raw[:, 2 * c + kk, :], wd_v[g * 2 + kk, :, c * 512:(c + 1) * 512])

            gate_up(U_F, 0)
            with sp.Fori(0, NG // 2) as i:
                u = i * 24 + (U_F + NK)
                gate_up(u, i * 2 + 1)
                down(u + 8, i * 2)
                gate_up(u + 12, i * 2 + 2)
                down(u + 20, i * 2 + 1)
            down(U_END - 4, NG - 1)
            for t in range(NT):
                sp.wait_ge(added, 2 * NT + t + 1)
                sp.dma_start(out_v[t], x1[:, t, :]).then_inc(stored, 16)
            sp.wait_ge(stored, 16 * NT)

        @block.gpsimd
        def _(pool):
            def split(u, u0, k, width, first=False, loads=None, hi=w_hi, lo=w_lo, used=None):
                s = k % RING
                w_used_up = u + (k - RING + 1) if used is None else used
                n = 16 * ((u0 + k) // RING + 1)
                pool.wait_ge(w_loaded[s], n if loads is None else loads * 16 + n)
                if not first:
                    pool.wait_ge(w_used, w_used_up)
                nc.gpsimd.tensor_tensor(hi[:, s, 0:width], raw[:, s, 0:width],
                                        zero[:, 0:1].broadcast_to([P, width]), ALU.add).then_inc(w_rounded, 1)
                pool.wait_ge(w_rounded, u + (k + 1 - (4 * NK if u0 >= U_Q else 0)))
                nc.gpsimd.tensor_tensor(lo[:, s, 0:width], raw[:, s, 0:width], hi[:, s, 0:width].bitcast(F32),
                                        ALU.subtract).then_inc(w_split, 1)

            pool.wait_ge(set_up, 1)
            for k in range(NK):
                split(U_Z, U_Z, k, ZW, k < RING)
            with pool.Fori(1, ZP) as c:
                for k in range(NK):
                    split(c * NK + U_Z, U_Z, k, ZW, loads=c * 2)
            pool.wait_ge(gb_in, 32)
            for t in range(NT):
                pool.wait_ge(gate_on, t + 1)
                g = z[:, t, C_RG:C_RG + RH * RD]
                nc.gpsimd.tensor_tensor(g, g, gain_b[:, 512:1024], ALU.mult).then_inc(gated, 1)
            pool.wait_ge(dk_v, 12)
            pool.wait_ge(sc_ready, NT * AH)
            for h in range(RH):
                pool.wait_ge(r_st, 2 * (h + 1))
                for f in range(2):
                    nc.gpsimd.tensor_tensor(qdec[f][:, h, :].rearrange("p (n i) -> p n i", n=NT),
                                            rqT[:, h, :].rearrange("p (n i) -> p n i", n=NT),
                                            qtab[:, h, f, :].unsqueeze(1).broadcast_to([P, NT, P]),
                                            ALU.mult).then_inc(r_qd, 1)
            for k in range(RING):
                split(U_O, U_O, k, 512)
            for t in range(NT):
                pool.wait_ge(r_n, 1 + RH * (t + 1))
                v = z[:, t, C_RQ:C_RQ + RH * RD]
                nc.gpsimd.tensor_tensor(v, v, z[:, t, C_RG:C_RG + RH * RD], ALU.mult).then_inc(mixed, 1)
            def output_units(u0):
                for k in range(RING if u0 == U_O else 0, NK):
                    split(u0, u0, k, 512)
                pool.wait_ge(summed, 2 * NT + NM)
                for k in range(RING):
                    split(u0 + NK, u0 + NK, k, 512, hi=w_hi2, lo=w_lo2, used=u0 + RING)
                for k in range(RING, NK):
                    split(u0 + NK, u0 + NK, k, 512, used=u0 + k + 1)

            def add_rows(n0, tiles=range(NT)):
                for t in tiles:
                    pool.wait_ge(r_post, n0 + t + 1)
                    if n0 == 0:
                        pool.wait_ge(x1_in[t], 16)
                    nc.gpsimd.tensor_tensor(x1[:, t, :], x1[:, t, :], y[:, t, :], ALU.add).then_inc(added, 1)

            output_units(U_O)
            add_rows(0, range(NT - 1))

            def mem_low(c, ks):
                for k in ks:
                    s = k % RING
                    pool.wait_ge(mem_rounded, c * NK + (k + 1))
                    nc.gpsimd.tensor_tensor(w_lo[:, s, :], raw[:, s, :], w_hi[:, s, :].bitcast(F32),
                                            ALU.subtract).then_inc(w_split, 1)

            mem_low(0, range(RING))
            add_rows(0, [NT - 1])
            mem_low(0, range(RING, NK))
            with pool.Fori(1, 4) as c:
                mem_low(c, range(NK))
            with pool.Fori(0, 2) as c:
                for k in range(NK):
                    split(c * NK + U_Q, U_Q, k, 512, loads=c * 2)
            output_units(U_XO)
            add_rows(NT)
            for k in range(NK):
                split(U_F, U_F, k, 512)
                if k == RING - 1:
                    pool.wait_ge(turned, TURNED["h3"] + 2 * NT)
                    for t in range(NT):
                        nc.gpsimd.memset(y[:, t, :], 0.0).then_inc(y_zero, 1)
            with pool.Fori(0, NG // 2) as i:
                for k in range(24):
                    split(i * 24 + (U_F + NK), U_F + NK, k, 512, loads=i * 6)
            for k in range(4):
                split(U_END - 4, U_END - 4, k, 512)
            add_rows(2 * NT)

        @block.tensor
        def _(pe):
            def transpose_to(b, col, src):
                return nc.tensor.transpose(ps[:, b, col:col + P], src, ident[:, :])

            def three(out, a_hi, a_lo, b_hi, b_lo, start, stop):
                nc.tensor.matmul(out, a_hi, b_hi, start=start, stop=False)
                nc.tensor.matmul(out, a_hi, b_lo, start=False, stop=False)
                return nc.tensor.matmul(out, a_lo, b_hi, start=False, stop=stop)

            def product(u, nbanks, width, bank_free, operands, b0=0, nk=NK, done=tile_done):
                for k in range(nk):
                    pe.wait_ge(w_split, u + (k + 1))
                    for t in range(nbanks):
                        if k == 0:
                            bank_free(t)
                        last = three(ps[:, b0 + t, 0:width], *operands(k, t), k == 0, k == nk - 1)
                        if t == nbanks - 1:
                            last.then_inc(w_used, 1)
                        elif k == nk - 1:
                            last.then_inc(done, 1)

            def rows_by_weights(hi, lo, width):
                def operands(k, t):
                    s = k % RING
                    return (hi[:, k, t * P:(t + 1) * P], lo[:, k, t * P:(t + 1) * P],
                            w_hi[:, s, 0:width], w_lo[:, s, 0:width])
                return operands

            def last_piece(u, seen, hi2, lo2):
                for t in range(NT):
                    pe.wait_ge(act_ev, seen + t + 1)
                    for k in range(NK):
                        if t == 0:
                            pe.wait_ge(w_split, u + k + 1)
                        hi, lo = (hi2, lo2) if k < RING else (w_hi, w_lo)
                        last = three(ps[:, t, :], t_hi[:, k, t * P:(t + 1) * P], t_lo[:, k, t * P:(t + 1) * P],
                                     hi[:, k % RING, :], lo[:, k % RING, :], k == 0, k == NK - 1)
                        if t == NT - 1:
                            last.then_inc(w_used, 1)
                        elif k == NK - 1:
                            last.then_inc(tile_done, 1)

            def turn_rows(t, srcs, b, ready, free):
                ready()
                for half in range(2):
                    free(half)
                    for j in range(4):
                        last = transpose_to(b + half, j * P, srcs(4 * half + j))
                    last.then_inc(turned, 1)

            pe.wait_ge(ident_in, 16)
            for t in range(NT):
                turn_rows(t, lambda j: z[:, t, j * P:(j + 1) * P], 2 * (t % 4),
                          lambda: pe.wait_ge(scaled, t + 1),
                          lambda half: pe.wait_ge(dve_ev, 2 * (t - 4) + half + 1) if t >= 4 else None)
            pe.wait_ge(dve_ev, DVE_EV["qk"])
            with pe.Fori(0, ZP) as c:
                product(c * NK + U_Z, NT, ZW,
                        lambda t: pe.wait_ge(act_ev, c * NT + (ACT_EV["z"] - NT + t + 1)),
                        rows_by_weights(t_hi, t_lo, ZW))

            groups = [(lambda t, j=j: z[:, t, C_Q + j * P:C_Q + (j + 1) * P], ROPE_A)
                      for j in range(G)]
            groups += [(lambda t: z[:, t, C_K:C_V], ROPE_A)]
            groups += [(lambda t, o=C_RQ + h * RD: z[:, t, o:o + RD], ROPE_R) for h in range(2 * RH)]
            pe.wait_ge(act_ev, ACT_EV["qk"])
            for i in range(2 * len(groups)):
                src, steps = groups[i // 2]
                pe.wait_ge(roped, steps)
                if i >= 8:
                    if i % 2 == 0:
                        pe.wait_ge(act_ev, ACT_EV["qk"] + (i - 8) // 2 + 1)
                    else:
                        pe.wait_ge(dve_ev, DVE_EV["qk"] + (i - 8) // 2 + 1)
                for j in range(4):
                    last = transpose_to(i % 8, j * P, src(4 * (i % 2) + j))
                last.then_inc(turned, 1)

            pe.wait_ge(act_ev, ACT_EV["c"])
            pe.wait_ge(dve_ev, DVE_EV["c"])

            def keys(n):
                return max(n - 1, 0), min(n + 2, NT)

            def scores(s):
                n, g = divmod(s, AKV)
                k0, k1 = keys(n)
                for j in range(G):
                    if s:
                        pe.wait_ge(w_max, G * (s - 1) + j + 1)
                    nc.tensor.matmul(ps[:, j, 0:(k1 - k0) * P], qT[g * AD:(g + 1) * AD, j, n * P:(n + 1) * P],
                                     kT[g * AD:(g + 1) * AD, k0 * P:k1 * P], start=True, stop=True).then_inc(sc_ready, 1)

            def copied(q):
                s, j = divmod(q, G)
                pe.wait_ge(w_pd if j % 2 else w_pa, 2 * s + j // 2 + 1)

            def turn_probs(s, j):
                n, g = divmod(s, AKV)
                k0, k1 = keys(n)
                q = G * s + j
                pe.wait_ge(w_exp, 5 * s + j + 1)
                if q >= 3:
                    copied(q - 3)
                for kb in range(k1 - k0):
                    last = transpose_to(4 + q % 3, kb * P, sm[:, s % 2, j, kb * P:(kb + 1) * P])
                last.then_inc(w_tr, 1)

            def values(s, j):
                n, g = divmod(s, AKV)
                k0, k1 = keys(n)
                copied(G * s + j)
                if g == 0 and j == 0 and n:
                    pe.wait_ge(w_a, n)
                h = g * G + j
                for kb in range(k1 - k0):
                    last = nc.tensor.matmul(ps[:, 7, h * AD:(h + 1) * AD], pTw[:, j, kb * P:(kb + 1) * P],
                                            z[:, k0 + kb, C_V + g * AD:C_V + (g + 1) * AD],
                                            start=kb == 0, stop=kb == k1 - k0 - 1)
                last.then_inc(w_pv, 1)

            steps = NT * AKV
            scores(0)
            for s in range(steps):
                if s + 1 < steps:
                    scores(s + 1)
                for j in range(3):
                    turn_probs(s, j)
                values(s, 0)
                turn_probs(s, 3)
                for j in range(1, G):
                    values(s, j)

            def chunk_products(h):
                for n in range(NT):
                    if n % 4 == 0 and h:
                        pe.wait_ge(r_sm, 2 * (h - 1) + n // 4 + 1)
                    if n == 0 and h == 0:
                        pe.wait_ge(w_max, NT * AH)
                    last = nc.tensor.matmul(ps[:, n // 4, (n % 4) * P:(n % 4 + 1) * P], rkT[:, h, n * P:(n + 1) * P],
                                            rqT[:, h, n * P:(n + 1) * P], start=True, stop=True)
                    if n % 4 == 3:
                        last.then_inc(r_st, 1)
                pe.wait_ge(r_vd, 2 * h + 2)
                if h == 0:
                    pe.wait_ge(w_pa, 2 * steps)
                    pe.wait_ge(w_pd, 2 * steps)
                else:
                    pe.wait_ge(r_scan, 14 * h)
                for n in range(NT):
                    nc.tensor.matmul(ps[:, 2 + n // 2, (n % 2) * 256:(n % 2 + 1) * 256],
                                     z[:, n, C_RK + h * RD:C_RK + (h + 1) * RD], vdec[:, n, :, :],
                                     start=True, stop=True).then_inc(r_kv, 1)

            def outputs(h):
                pe.wait_ge(r_qd, 2 * h + 2)
                pe.wait_ge(r_scan, 14 * (h + 1))
                for n in range(NT):
                    if n % 4 == 0:
                        pe.wait_ge(r_sm, 2 * h + n // 4 + 1)
                        if h:
                            pe.wait_ge(r_yc, 2 * (h - 1) + n // 4 + 1)
                        elif n == 0:
                            pe.wait_ge(w_a, NT)
                    o = ps[:, 6 + n // 4, (n % 4) * P:(n % 4 + 1) * P]
                    c = slice(n * P, (n + 1) * P)
                    terms = [(smt[h % 2][:, n, :], z[:, n, C_RV + h * RD:C_RV + (h + 1) * RD])]
                    if n:
                        terms.append((qdec[0][:, h, c], states[:, h % 2, n, 0, :]))
                    if n < NT - 1:
                        terms.append((qdec[1][:, h, c], states[:, h % 2, n, 1, :]))
                    for i, (a, b) in enumerate(terms):
                        last = nc.tensor.matmul(o, a, b, start=i == 0, stop=i == len(terms) - 1)
                    last.then_inc(r_y, 1)

            chunk_products(0)
            for h in range(RH):
                if h + 1 < RH:
                    chunk_products(h + 1)
                outputs(h)

            for t in range(NT):
                turn_rows(t, lambda j: z[:, t, (C_Q if j < 4 else C_RQ) + (j % 4) * P:][:, 0:P], 2 * (t % 4),
                          lambda: (pe.wait_ge(a_n, t + 1), pe.wait_ge(mixed, t + 1)),
                          lambda half: pe.wait_ge(dve_ev, DVE_EV["c"] + 2 * (t - 4) + half + 1) if t >= 4 else (
                              pe.wait_ge(r_yc, 2 * RH)))
            pe.wait_ge(dve_ev, DVE_EV["mem"])
            product(U_O, NT, 512, lambda t: pe.wait_ge(act_ev, ACT_EV["o"] - NT + t + 1),
                    rows_by_weights(t_hi, t_lo, 512))
            last_piece(U_O + NK, ACT_EV["o"], w_hi2, w_lo2)

            def turn_tile(stage, n0, t):
                turn_rows(t, lambda j: y[:, t, j * P:(j + 1) * P], 4 + 2 * (t % 2),
                          lambda: pe.wait_ge(scaled, n0 + t + 1),
                          lambda half: pe.wait_ge(dve_ev, DVE_EV[stage] + 2 * (t - 2) + half + 1) if t >= 2 else None)

            pe.wait_ge(act_ev, ACT_EV["mem"])
            for t in range(NM):
                turn_rows(t, lambda j: mem_t[:, t, j * P:(j + 1) * P], 4 + 2 * t,
                          lambda: pe.wait_ge(scaled, NT + t + 1), lambda half: None)
            pe.wait_ge(dve_ev, DVE_EV["h2"])
            for c in range(4):
                product(c * NK + U_KV, NM, 512, lambda t: pe.wait_ge(act_ev, kv_seen(c - 2, t)) if c >= 2 else None,
                        rows_by_weights(m_hi, m_lo, 512), b0=2 * (c % 2))
                turn_tile("h2", NT + NM, 2 * c)
                turn_tile("h2", NT + NM, 2 * c + 1)
            pe.wait_ge(act_ev, kv_seen(3, 1))
            for i in range(4):
                for j in range(4):
                    kt, mt = divmod(4 * i + j, NM)
                    last = transpose_to(i, j * P, kst[:, mt, kt * P:(kt + 1) * P])
                last.then_inc(turned, 1)

            pe.wait_ge(dve_ev, DVE_EV["h3"])
            pe.wait_ge(act_ev, ACT_EV["q"])

            def features_by_rows(k, t):
                s, m, half = k % RING, t // 2, t % 2
                return (w_hi[:, s, m * P:(m + 1) * P], w_lo[:, s, m * P:(m + 1) * P],
                        t_hi[:, k, half * 512:(half + 1) * 512], t_lo[:, k, half * 512:(half + 1) * 512])

            with pe.Fori(0, 2) as c:
                product(c * NK + U_Q, NT, 512,
                        lambda t: pe.wait_ge(act_ev, c * NT + (ACT_EV["q"] - NT + t + 1)),
                        features_by_rows)

            pe.wait_ge(act_ev, ACT_EV["xo"])

            def mem_scores(t):
                if t >= 2:
                    pe.wait_ge(x_exp, XH * (t - 1))
                for h in range(XH):
                    o = ps[:, 2 * (t % 2) + h // 2, (h % 2) * N_MEM:(h % 2 + 1) * N_MEM]
                    for kk in range(2):
                        last = nc.tensor.matmul(o, qX[:, 2 * h + kk, t * P:(t + 1) * P], kM[:, 2 * h + kk, :],
                                                start=kk == 0, stop=kk == 1)
                last.then_inc(x_sc, 1)

            def mem_turn(t):
                pe.wait_ge(x_nrm, 2 * t + 2)
                for b in range(2):
                    if t:
                        pe.wait_ge(x_pd if b else x_pa, t)
                    for j in range(4):
                        h, mm = 2 * b + j // 2, j % 2
                        last = transpose_to(4 + b, j * P, px[:, t % 2, h, mm * P:(mm + 1) * P])
                    last.then_inc(x_tr, 1)

            def mem_values(half):
                pe.wait_ge(x_pa, 4 * (half + 1))
                pe.wait_ge(x_pd, 4 * (half + 1))
                for d in range(NK):
                    n = NK * half + d
                    if n >= 2:
                        pe.wait_ge(x_lo, n - 1)
                    for mm in range(NM):
                        last = nc.tensor.matmul(ps[:, 6 + d % 2, :], vM[:, mm, d * P:(d + 1) * P], pTx[:, mm, d // 2, :],
                                                start=mm == 0, stop=mm == NM - 1)
                    last.then_inc(x_pv, 1)

            mem_scores(0)
            for t in range(NT):
                if t + 1 < NT and t != 4:
                    mem_scores(t + 1)
                mem_turn(t)
                if t == 3:
                    mem_scores(5)
                if t % 4 == 3:
                    mem_values(t // 4)

            pe.wait_ge(x_lo, 2 * NK)
            pe.wait_ge(x_exp, XH * NT)
            product(U_XO, NT, 512, lambda t: pe.wait_ge(act_ev, ACT_EV["xo"] - NT + t + 1),
                    rows_by_weights(t_hi, t_lo, 512))
            last_piece(U_XO + NK, ACT_EV["xo"], w_hi2, w_lo2)
            pe.wait_ge(act_ev, ACT_EV["h3"])
            for t in range(NT):
                turn_tile("h3", 2 * NT + NM, t)

            pe.wait_ge(dve_ev, DVE_EV["end"])

            def gate_up(u, seen=None):
                def operands(k, t):
                    s, ch, half, up = k % RING, t // 4, t // 2 % 2, t % 2
                    w = slice(up * FG + ch * P, up * FG + (ch + 1) * P)
                    return (w_hi[:, s, w], w_lo[:, s, w],
                            t_hi[:, k, half * 512:(half + 1) * 512], t_lo[:, k, half * 512:(half + 1) * 512])
                product(u, 8, 512, lambda t: None if seen is None else pe.wait_ge(dve_ev, seen + (t + 1)), operands)

            def down(u, buf, low, free):
                pe.wait_ge(f_low, low)
                for c in range(2):
                    def operands(k, t):
                        s = 2 * c + k
                        return (f_hi[:, buf, k, t * P:(t + 1) * P], f_lo[:, buf, k, t * P:(t + 1) * P],
                                w_hi[:, s, :], w_lo[:, s, :])
                    product(u + 2 * c, NT, 512, lambda t: pe.wait_ge(dve_ev, free(c, t)), operands, nk=2, done=f_bank)

            gate_up(U_F)
            pe.wait_ge(dve_ev, F_EV)
            with pe.Fori(0, NG // 2) as i:
                for odd in range(2):
                    u = i * 24 + (U_F + NK + 12 * odd)
                    start = i * 40 + (F_EV + 20 * odd)
                    gate_up(u, start - 8)
                    down(u + NK, odd, i * 8 + 4 * (odd + 1),
                         lambda c, t: start + ((t // 2 + 1) if c == 0 else (4 + t + 1)))
            pe.wait_ge(f_low, 4 * NG)
            for n in range(2 * NT):
                t, c = divmod(n, 2)
                pe.wait_ge(dve_ev, F_EV + 20 * (NG - 1) + n - 8 + 1)
                for k in range(2):
                    s = 2 * c + k
                    if t == 0:
                        pe.wait_ge(w_split, U_END - 4 + s + 1)
                    last = three(ps[:, n % 8, :], f_hi[:, (NG - 1) % 2, k, t * P:(t + 1) * P],
                                 f_lo[:, (NG - 1) % 2, k, t * P:(t + 1) * P], w_hi[:, s, :], w_lo[:, s, :], k == 0, k == 1)
                last.then_inc(f_bank, 1)

        @block.scalar
        def _(act):
            def square_root(i, src, scratch, n, ready):
                ready()
                nc.scalar.activation(scratch, src, ACT.Square, accum_out=ss[:, i:i + 1]).then_inc(summed, 1)
                act.wait_ge(summed, i + 1)
                nc.scalar.activation(rms[:, i:i + 1], ss[:, i:i + 1], ACT.Sqrt, bias=eps[:, 0:1],
                                     scale=1.0 / n).then_inc(rooted, 1)

            def hi_parts(n, dst, col):
                for half in range(2):
                    act.wait_ge(turned, n + half + 1)
                    b = turn_bank(n + half)
                    nc.scalar.activation(dst[:, 4 * half:4 * half + 4, col:col + P],
                                         bank(b).rearrange("p (k i) -> p k i", k=4), ACT.Copy).then_inc(act_ev, 1)

            def tile_ready(stage, c, t, nbanks, u):
                if t < nbanks - 1:
                    act.wait_ge(tile_done, c * (nbanks - 1) + (TILES[stage] + t + 1))
                else:
                    act.wait_ge(w_used, u + NK)

            act.dma_start(gain_a[:, :], rows(norm_mix_pre)).then_inc(ga_in, 16)
            act.dma_start(ident[:, :], identity).then_inc(ident_in, 16)
            act.wait_ge(set_up, 3)
            for t in range(NT):
                square_root(t, z[:, t, 0:D], z[:, t, D:2 * D], D, lambda: act.wait_ge(x_in[t], 16))
                if t:
                    hi_parts(TURNED["x"] + 2 * (t - 1), t_hi, (t - 1) * P)
            hi_parts(TURNED["x"] + 2 * (NT - 1), t_hi, (NT - 1) * P)

            act.dma_start(sink[:, :], rows(attn_sink)).then_inc(c_in, 16)
            act.dma_start(dec[:, 0:RH], rows(ret_decay_fwd)).then_inc(c_in, 16)
            act.dma_start(dec[:, RH:2 * RH], rows(ret_decay_bwd)).then_inc(c_in, 16)
            act.dma_start(vpow[:, :], value_powers).then_inc(c_in, 16)
            act.dma_start(ropet[:, :], rope_tables).then_inc(rope_in, 16)
            act.dma_start(band[:, :], band_mask).then_inc(band_in, 16)
            act.dma_start(gain_b[:, 0:512], rows(attn_out_norm)).then_inc(gb_in, 16)
            act.dma_start(gain_b[:, 512:1024], rows(ret_gn)).then_inc(gb_in, 16)

            act.wait_ge(scaled, NT)
            act.dma_start(gain_a[:, :], rows(norm_mix_post)).then_inc(ga_in, 16)
            with act.Fori(0, ZP - 1) as c:
                for t in range(NT):
                    tile_ready("z", c, t, NT, c * NK + U_Z)
                    nc.scalar.activation(z[:, t, bass.ds(c * ZW, ZW)], bank(t, ZW), ACT.Copy).then_inc(act_ev, 1)
            act.wait_ge(roped, ROPE_R)
            act.dma_start(powers[:, :], decay_powers).then_inc(pow_in, 16)

            act.wait_ge(c_in, 16 * 4)
            nc.scalar.activation(dec_t[:, 0, :], dec[:, :], ACT.Abs).then_inc(dk_a, 1)
            act.wait_ge(dk_a, 1)
            nc.scalar.activation(dec_t[:, 1, :], dec_t[:, 0, :], ACT.Exp, scale=-1.0).then_inc(dk_a, 1)
            act.wait_ge(dk_a, 2)
            nc.scalar.activation(dec_t[:, 2, :], dec_t[:, 1, :], ACT.Ln, bias=one[:, 0:1]).then_inc(dk_a, 1)
            act.wait_ge(dk_v, 9)
            nc.scalar.activation(dtab[:, :, :], dtab[:, :, :], ACT.Exp).then_inc(dk_a, 1)
            act.wait_ge(dk_v, 10)
            nc.scalar.activation(vtab[:, :], vtab[:, :], ACT.Exp).then_inc(dk_a, 1)
            nc.scalar.activation(cdec[:, :], lg[:, :], ACT.Exp, scale=float(P)).then_inc(dk_a, 1)
            act.wait_ge(pow_in, 16)
            for h in range(RH):
                for f in range(2):
                    nc.scalar.activation(qtab[:, h, f, :], powers[:, (2 + f) * P:(3 + f) * P], ACT.Exp,
                                         scale=lg[:, f * RH + h:f * RH + h + 1]).then_inc(dk_a, 1)

            for t in range(NT):
                tile_ready("z", ZP - 1, t, NT, (ZP - 1) * NK + U_Z)
                nc.scalar.activation(z[:, t, (ZP - 1) * ZW:ZP * ZW], bank(t, ZW), ACT.Copy).then_inc(act_ev, 1)
            for i in range(0, 26, 2):
                act.wait_ge(turned, TURNED["qk"] + i + 1)
                nc.scalar.activation(qk_dst(i), bank(i % 8), ACT.Copy).then_inc(act_ev, 1)
            act.wait_ge(act_ev, ACT_EV["qk"])
            for t in range(NT):
                g = z[:, t, C_RG:C_RG + RH * RD]
                nc.scalar.activation(g, g, ACT.Silu).then_inc(gate_on, 1)

            def exponentials(s, heads):
                n, g = divmod(s, AKV)
                nk = width(n)
                for j in heads:
                    act.wait_ge(w_small, 2 * s + 1)
                    h = g * G + j
                    p = sm[:, s % 2, j, 0:nk]
                    nc.scalar.activation(p, p, ACT.Exp, bias=wnm[:, n, h:h + 1], scale=A_SCALE,
                                         accum_out=wrs[:, n, h:h + 1]).then_inc(w_exp, 1)

            def sink_term(s):
                n, g = divmod(s, AKV)
                act.wait_ge(w_small, 2 * s + 2)
                nc.scalar.activation(wes[:, n, g * G:(g + 1) * G], wds[:, n, g * G:(g + 1) * G],
                                     ACT.Exp).then_inc(w_exp, 1)

            def copy_probs(s, j):
                q = G * s + j
                act.wait_ge(w_tr, q + 1)
                if s:
                    act.wait_ge(w_pv, q - G + 1)
                nk = width(s // AKV)
                nc.scalar.activation(pTw[:, j, 0:nk], bank(4 + q % 3, nk), ACT.Copy).then_inc(w_pa, 1)

            steps = NT * AKV
            act.wait_ge(dk_v, 12)
            exponentials(0, range(G))
            sink_term(0)
            for s in range(steps):
                more = s + 1 < steps
                copy_probs(s, 0)
                if more:
                    exponentials(s + 1, (0, 1))
                copy_probs(s, 2)
                if more:
                    exponentials(s + 1, (2, 3))
                    sink_term(s + 1)

            def decayed_values(h):
                act.wait_ge(r_kv, NT * h) if h else act.wait_ge(w_tr, G * steps)
                for f in range(2):
                    nc.scalar.activation(vdec[:, :, f, :], z[:, :, C_RV + h * RD:C_RV + (h + 1) * RD], ACT.Copy,
                                         scale=vtab[:, f * RH + h:f * RH + h + 1]).then_inc(r_vd, 1)

            decayed_values(0)
            decayed_values(1)
            for h in range(RH):
                if h == 0:
                    for t in range(NT):
                        square_root(NT + t, z[:, t, 0:512], junk_c[:, 0:512], 512, lambda: act.wait_ge(w_a, t + 1))
                if h + 2 < RH:
                    decayed_values(h + 2)
                for b in range(2):
                    act.wait_ge(r_y, NT * h + 4 * (b + 1))
                    nc.scalar.activation(z[:, 4 * b:4 * b + 4, C_RQ + h * RD:C_RQ + (h + 1) * RD],
                                         bank(6 + b).rearrange("p (n e) -> p n e", n=4), ACT.Copy).then_inc(r_yc, 1)
            act.wait_ge(r_qd, 2 * RH)
            act.dma_start(mem_t[:, :, :], mem[0].rearrange("(m p) d -> p m d", p=P)).then_inc(mem_in, 16)
            act.wait_ge(r_bn, 2 * RH * NT)
            nc.scalar.activation(rsd[:, :], mv[:, :, 1], ACT.Sqrt, bias=eps[:, 0:1]).then_inc(r_rt, 1)
            for t in range(NT):
                hi_parts(TURNED["c"] + 2 * t, t_hi, t * P)

            act.wait_ge(a_n, NT)
            act.wait_ge(mixed, NT)
            act.wait_ge(turned, TURNED["mem"])
            act.dma_start(gain_b[:, :], rows(norm_mem)).then_inc(gb_in, 16)
            for t in range(NT):
                act.dma_start(x1[:, t, :], x_v[t]).then_inc(x1_in[t], 16)
            for m in range(NM):
                square_root(2 * NT + m, mem_t[:, m, :], squares, D,
                            lambda: act.wait_ge(mem_in, 16))
            act.wait_ge(scaled, NT + NM)
            act.dma_start(gain_b[:, :], rows(norm_xa_pre)).then_inc(gb_in, 16)

            def product_out(stage, u0, dst):
                with act.Fori(0, 2) as c:
                    for t in range(NT):
                        tile_ready(stage, c, t, NT, c * NK + u0)
                        nc.scalar.activation(dst(c, t), bank(t), ACT.Copy).then_inc(act_ev, 1)

            done = 0
            rounds = 0

            def round_units(n):
                nonlocal rounds
                for _ in range(min(n, 4 * NK - rounds)):
                    u, slot = U_KV + rounds, (U_KV + rounds) % RING
                    act.wait_ge(w_loaded[slot], 16 * (u // RING + 1))
                    act.wait_ge(w_used, u - RING + 1)
                    nc.scalar.activation(w_hi[:, slot, :], raw[:, slot, :], ACT.Copy).then_inc(mem_rounded, 1)
                    rounds += 1

            def sums(seq, i0, items, scratch, added0, extra=0):
                for i in items:
                    round_units(extra)
                    kind, t = seq[i]
                    if kind == "post":
                        square_root(i0 + i, y[:, t, :], scratch, D, lambda: None)
                    else:
                        square_root(i0 + i, x1[:, t, :], scratch, D, lambda: act.wait_ge(added, added0 + t + 1))

            def until(t, i0, scr, added0, extra=0):
                nonlocal done
                end = SEQ.index(("pre", min(t, NT - 1))) + 1
                sums(SEQ, i0, range(done, end), scr, added0, extra)
                done = max(done, end)

            def last_piece_out(stage, i0, scr, added0):
                nonlocal done
                u0 = U_O if stage == "o" else U_XO
                for t in range(NT):
                    tile_ready(stage, 0, t, NT, u0)
                    nc.scalar.activation(y[:, t, 0:512], bank(t), ACT.Copy).then_inc(act_ev, 1)
                done = 0
                for t in range(NT):
                    tile_ready(stage, 1, t, NT, u0 + NK)
                    nc.scalar.activation(y[:, t, 512:1024], bank(t), ACT.Copy).then_inc(act_ev, 1)
                    act.wait_ge(act_ev, ACT_EV[stage] + NT + t + 1)
                    end = SEQ.index(("pre", t - 1)) + 1 if t else 1
                    if t == NT - 1:
                        end = done if stage == "o" else done + 1
                    sums(SEQ, i0, range(done, end), scr, added0)
                    done = end

            last_piece_out("o", I_H2, squares, 0)
            round_units(4)
            for m in range(NM):
                hi_parts(TURNED["mem"] + 2 * m, m_hi, m * P)
            until(NT - 1, I_H2, squares, 0)
            round_units(4)
            for c in range(4):
                round_units(4)
                for t in range(NM):
                    if t == 0:
                        act.wait_ge(tile_done, TILES["kv"] + c + 1)
                    else:
                        act.wait_ge(w_used, U_KV + NK * (c + 1))
                    dst = kst if c < 2 else vM
                    nc.scalar.activation(dst[:, t, (c % 2) * 512:(c % 2 + 1) * 512], bank(2 * (c % 2) + t),
                                         ACT.Copy).then_inc(act_ev, 1)
                for t in (2 * c, 2 * c + 1):
                    hi_parts(TURNED["h2"] + 2 * t, t_hi, t * P)
                round_units(NK * (c + 2) - rounds)
            for i in range(4):
                act.wait_ge(turned, TURNED["k"] + i + 1)
                nc.scalar.activation(kM[:, 2 * i:2 * i + 2, :], bank(i).rearrange("p (k m) -> p k m", k=2),
                                     ACT.Copy).then_inc(act_ev, 1)
            act.wait_ge(added, NT)
            act.dma_start(gain_a[:, :], rows(norm_xa_post)).then_inc(ga_in, 16)
            act.wait_ge(scaled, 2 * NT + NM)
            act.dma_start(gain_b[:, :], rows(norm_ffn_pre)).then_inc(gb_in, 16)

            product_out("q", U_Q, lambda c, t: qX[:, bass.ds(c * 4 + t // 2, 1), (t % 2) * 512:(t % 2 + 1) * 512])

            def mem_exp(t):
                act.wait_ge(x_mx, 2 * t + 2)
                if t >= 2:
                    act.wait_ge(x_tr, 2 * (t - 1))
                for h in range(XH):
                    nc.scalar.activation(px[:, t % 2, h, :], ps[:, 2 * (t % 2) + h // 2, (h % 2) * N_MEM:(h % 2 + 1) * N_MEM],
                                         ACT.Exp, bias=wnm[:, t, h:h + 1], scale=X_SCALE,
                                         accum_out=wrs[:, t, h:h + 1]).then_inc(x_exp, 1)

            mem_exp(0)
            for t in range(NT):
                act.wait_ge(x_tr, 2 * t + 1)
                if t >= 4:
                    act.wait_ge(x_pv, NK)
                nc.scalar.activation(pTx[:, :, 0:2, (t % 4) * P:(t % 4 + 1) * P],
                                     bank(4).rearrange("p (h m i) -> p m h i", h=2, m=2), ACT.Copy).then_inc(x_pa, 1)
                if t + 1 < NT:
                    mem_exp(t + 1)
                if t % 4 == 3:
                    half = t // 4
                    for d in range(NK):
                        act.wait_ge(x_pv, NK * half + d + 1)
                        nc.scalar.activation(t_hi[:, d, half * 512:(half + 1) * 512], bank(6 + d % 2),
                                             ACT.Copy).then_inc(x_hi, 1)

            last_piece_out("xo", I_H3, squares, NT)
            for t in range(NT):
                hi_parts(TURNED["h3"] + 2 * t, t_hi, t * P)
                if t == 0:
                    sums(SEQ, I_H3, range(done, done + 1), squares, NT)
                    done += 1
                if t == 2:
                    until(NT - 1, I_H3, squares, NT)
            act.wait_ge(added, 2 * NT)
            act.dma_start(gain_a[:, :], rows(norm_ffn_post)).then_inc(ga_in, 16)

            def group(g, seen, first=False):
                def silu(p):
                    act.wait_ge(tile_done, g * 7 + (TILES["f"] + 2 * p + 1))
                    if not first:
                        act.wait_ge(f_low, g * 4 + (p - 3))
                    nc.scalar.activation(gs[:, p, :], bank(2 * p), ACT.Silu).then_inc(f_silu, 1)

                def high(p):
                    act.wait_ge(dve_ev, seen + (p + 1))
                    nc.scalar.activation(f_hi[:, buf, p // 2, (p % 2) * 512:(p % 2 + 1) * 512], gs[:, p, :],
                                         ACT.Copy).then_inc(f_high, 1)
                silu(0)
                silu(1)
                high(0)
                silu(2)
                high(1)
                silu(3)
                high(2)
                high(3)

            buf = 0
            group(0, DVE_EV["end"], True)
            with act.Fori(0, NG // 2) as i:
                for buf in (1, 0):
                    group(i * 2 + (2 - buf), i * 40 + (F_EV + 20 * (1 - buf)))
            for t in range(NT):
                square_root(I_END + t, y[:, t, :], squares, D,
                            lambda: act.wait_ge(dve_ev, F_EV + 20 * (NG - 1) + 2 * t + 2))

        @block.vector
        def _(dve):
            def invert(i):
                dve.wait_ge(rooted, i + 1)
                nc.vector.reciprocal(rstd[:, i:i + 1], rms[:, i:i + 1]).then_inc(inverted, 1)
                dve.wait_ge(inverted, i + 1)

            def lo_parts(hi_count, n, hi, lo, col):
                for half in range(2):
                    dve.wait_ge(act_ev, hi_count + half + 1)
                    b = turn_bank(n + half)
                    nc.vector.tensor_tensor(lo[:, 4 * half:4 * half + 4, col:col + P],
                                            bank(b).rearrange("p (k i) -> p k i", k=4),
                                            hi[:, 4 * half:4 * half + 4, col:col + P].bitcast(F32),
                                            ALU.subtract).then_inc(dve_ev, 1)

            nc.vector.memset(zero[:, :], 0.0).then_inc(set_up, 1)
            nc.vector.memset(eps[:, :], EPS).then_inc(set_up, 1)
            nc.vector.memset(one[:, :], 1.0).then_inc(set_up, 1)

            dve.wait_ge(ga_in, 16)
            for t in range(NT):
                invert(t)
                nc.vector.scalar_tensor_tensor(out=z[:, t, 0:D], in0=z[:, t, 0:D], scalar=rstd[:, t:t + 1],
                                               in1=gain_a[:, :], op0=ALU.mult, op1=ALU.mult).then_inc(scaled, 1)
                if t:
                    lo_parts(ACT_EV["x"] + 2 * (t - 1), TURNED["x"] + 2 * (t - 1), t_hi, t_lo, (t - 1) * P)
            lo_parts(ACT_EV["x"] + 2 * (NT - 1), TURNED["x"] + 2 * (NT - 1), t_hi, t_lo, (NT - 1) * P)

            dve.wait_ge(rope_in, 16)
            n = 0
            for c0, c1, d, cos, sin, pieces in ((C_Q, C_V, AD, cos_a, sin_a, 2), (C_RQ, C_RV, RD, cos_r, sin_r, 6)):
                heads = (c1 - c0) // d
                a = rope_a[:, 0:c1 - c0].rearrange("p (h two d) -> p h two d", h=heads, two=2)
                b = rope_b[:, 0:c1 - c0].rearrange("p (h two d) -> p h two d", h=heads, two=2)
                for t in range(NT):
                    dve.wait_ge(act_ev, ACT_EV["z"] + NT * (pieces - 1) + t + 1)
                    if n:
                        dve.wait_ge(roped, n)
                    v = z[:, t, c0:c1].rearrange("p (h two d) -> p h two d", h=heads, two=2)
                    cb = cos[:, t, :].unsqueeze(1).broadcast_to([P, 2 * heads, d // 2])
                    sb_ = sin[:, t, :].unsqueeze(1).broadcast_to([P, heads, d // 2])
                    nc.vector.tensor_tensor(a.rearrange("p h two d -> p (h two) d"),
                                            v.rearrange("p h two d -> p (h two) d"), cb, ALU.mult).then_inc(roped, 1)
                    nc.vector.tensor_tensor(b[:, :, 0, :], v[:, :, 1, :], sb_, ALU.mult).then_inc(roped, 1)
                    nc.vector.tensor_tensor(b[:, :, 1, :], v[:, :, 0, :], sb_, ALU.mult).then_inc(roped, 1)
                    dve.wait_ge(roped, n + 3)
                    outs = [(0, heads, v)]
                    if d == AD:
                        q = z[:, t, C_Q:C_K].rearrange("p (j g two d) -> p g j two d", g=AKV, j=G, two=2)
                        outs = [(g * G, (g + 1) * G, q[:, g, :, :, :]) for g in range(AKV)] + [(AH, heads, v[:, AH:heads, :, :])]
                    for h0, h1, o in outs:
                        nc.vector.tensor_tensor(o[:, :, 0, :], a[:, h0:h1, 0, :], b[:, h0:h1, 0, :],
                                                ALU.subtract).then_inc(roped, 1)
                        nc.vector.tensor_tensor(o[:, :, 1, :], a[:, h0:h1, 1, :], b[:, h0:h1, 1, :],
                                                ALU.add).then_inc(roped, 1)
                    n += 3 + 2 * len(outs)
            dve.wait_ge(c_in, 16 * 4)
            nc.vector.tensor_scalar(nsink[:, :], sink[:, :], -1.0, None, ALU.mult).then_inc(w_den, 1)
            dve.wait_ge(dk_a, 3)
            nc.vector.scalar_tensor_tensor(out=lg[:, :], in0=dec[:, :], scalar=0.0, in1=dec_t[:, 2, :],
                                           op0=ALU.min, op1=ALU.subtract).then_inc(dk_v, 1)
            dve.wait_ge(pow_in, 16)
            dve.wait_ge(dk_v, 1)
            for h in range(RH):
                nc.vector.tensor_scalar(dtab[:, h, :], powers[:, P:2 * P], lg[:, RH + h:RH + h + 1], None,
                                        ALU.mult).then_inc(dk_v, 1)
                dve.wait_ge(dk_v, 2 + 2 * h)
                nc.vector.scalar_tensor_tensor(out=dtab[:, h, :], in0=powers[:, 0:P], scalar=lg[:, h:h + 1],
                                               in1=dtab[:, h, :], op0=ALU.mult, op1=ALU.add).then_inc(dk_v, 1)
            nc.vector.tensor_tensor(vtab[:, :], vpow[:, :], lg[:, :], ALU.mult).then_inc(dk_v, 1)
            dve.wait_ge(dk_a, 4)
            nc.vector.tensor_scalar(dtab[:, :, :], dtab[:, :, :], R_SCALE, None, ALU.mult).then_inc(dk_v, 1)
            dve.wait_ge(dk_a, 14)
            nc.vector.tensor_scalar(qtab[:, :, :, :], qtab[:, :, :, :], R_SCALE, None, ALU.mult).then_inc(dk_v, 1)

            for i in range(1, 26, 2):
                dve.wait_ge(turned, TURNED["qk"] + i + 1)
                nc.vector.tensor_copy(qk_dst(i), bank(i % 8)).then_inc(dve_ev, 1)

            def maxima(s):
                n, g = divmod(s, AKV)
                nk = width(n)
                off = P if n == 0 else 0
                for j in range(G):
                    q = G * s + j
                    h = g * G + j
                    dve.wait_ge(sc_ready, q + 1)
                    if s >= 2:
                        dve.wait_ge(w_tr, G * (s - 2) + j + 1)
                    nc.vector.tensor_tensor_reduce(sm[:, s % 2, j, 0:nk], bank(j, nk), band[:, off:off + nk],
                                                   1.0, -3.0e38, ALU.add, ALU.max, wmx[:, n, h:h + 1]).then_inc(w_max, 1)
                dve.wait_ge(w_max, G * (s + 1))
                hs = slice(g * G, (g + 1) * G)
                nc.vector.scalar_tensor_tensor(out=wnm[:, n, hs], in0=wmx[:, n, hs], scalar=-A_SCALE, in1=nsink[:, hs],
                                               op0=ALU.mult, op1=ALU.min).then_inc(w_small, 1)
                dve.wait_ge(w_small, 2 * s + 1)
                nc.vector.tensor_tensor(wds[:, n, hs], sink[:, hs], wnm[:, n, hs], ALU.add).then_inc(w_small, 1)

            def copy_probs(s, j):
                q = G * s + j
                dve.wait_ge(w_tr, q + 1)
                if s:
                    dve.wait_ge(w_pv, q - G + 1)
                nk = width(s // AKV)
                nc.vector.tensor_copy(pTw[:, j, 0:nk], bank(4 + q % 3, nk)).then_inc(w_pd, 1)

            steps = NT * AKV
            dve.wait_ge(band_in, 16)
            dve.wait_ge(w_den, 1)
            maxima(0)
            for s in range(steps):
                if s + 1 < steps:
                    maxima(s + 1)
                copy_probs(s, 1)
                copy_probs(s, 3)
                if s % AKV == AKV - 1:
                    n = s // AKV
                    dve.wait_ge(w_exp, 5 * (s + 1))
                    nc.vector.tensor_tensor(wden[:, n, :], wrs[:, n, :], wes[:, n, :], ALU.add).then_inc(w_den, 1)
                    dve.wait_ge(w_den, 2 * n + 2)
                    nc.vector.reciprocal(wrd[:, n, :], wden[:, n, :]).then_inc(w_den, 1)
                    dve.wait_ge(w_den, 2 * n + 3)
                    dve.wait_ge(w_pv, G * (s + 1))
                    nc.vector.tensor_tensor(z[:, n, C_Q:C_K].rearrange("p (h d) -> p h d", h=AH),
                                            bank(7).rearrange("p (h d) -> p h d", h=AH),
                                            wrd[:, n, :].unsqueeze(2).broadcast_to([P, AH, AD]), ALU.mult).then_inc(w_a, 1)

            def decay_scores(h):
                for b in range(2):
                    dve.wait_ge(r_st, 2 * h + b + 1)
                    if h >= 2:
                        dve.wait_ge(r_y, NT * (h - 1))
                    nc.vector.tensor_tensor(smt[h % 2][:, 4 * b:4 * b + 4, :], bank(b).rearrange("p (n i) -> p n i", n=4),
                                            dtab[:, h, :].unsqueeze(1).broadcast_to([P, 4, P]), ALU.mult).then_inc(r_sm, 1)

            def recurrences(h):
                k = 14 * h
                for i in range(NT - 1):
                    for f, n in ((0, i), (1, NT - 1 - i)):
                        dst = states[:, h % 2, n + 1 if f == 0 else n - 1, f, :]
                        prod = ps[:, 2 + n // 2, (n % 2) * 256 + f * RD:(n % 2) * 256 + (f + 1) * RD]
                        dve.wait_ge(r_kv, NT * h + n // 2 * 2 + 2)
                        if i == 0:
                            nc.vector.tensor_copy(dst, prod).then_inc(r_scan, 1)
                        else:
                            dve.wait_ge(r_scan, k - 1)
                            nc.vector.scalar_tensor_tensor(out=dst, in0=states[:, h % 2, n, f, :],
                                                           scalar=cdec[:, f * RH + h:f * RH + h + 1], in1=prod,
                                                           op0=ALU.mult, op1=ALU.add).then_inc(r_scan, 1)
                        k += 1

            def statistics(h):
                k = 2 * NT * h
                for n in range(NT):
                    dve.wait_ge(r_yc, 2 * h + n // 4 + 1)
                    nc.vector.bn_stats(st6[:, h * NT + n, :], z[:, n, C_RQ + h * RD:C_RQ + (h + 1) * RD]).then_inc(r_bn, 1)
                for n in range(NT):
                    dve.wait_ge(r_bn, k + n + 1)
                    nc.vector.bn_aggr(mv[:, h * NT + n, :], st6[:, h * NT + n, :]).then_inc(r_bn, 1)

            dve.wait_ge(dk_v, 12)
            dve.wait_ge(gb_in, 32)
            for h in range(RH):
                decay_scores(h)
                recurrences(h)
                for t in range(2 * h, 2 * h + 2):
                    invert(NT + t)
                    a = z[:, t, 0:512]
                    nc.vector.scalar_tensor_tensor(out=a, in0=a, scalar=rstd[:, NT + t:NT + t + 1],
                                                   in1=gain_b[:, 0:512], op0=ALU.mult, op1=ALU.mult).then_inc(a_n, 1)
                if h:
                    statistics(h - 1)
            statistics(RH - 1)
            dve.wait_ge(r_rt, 1)
            nc.vector.reciprocal(rrs[:, :], rsd[:, :]).then_inc(r_n, 1)
            dve.wait_ge(r_n, 1)
            for t in range(NT):
                for h in range(RH):
                    v = z[:, t, C_RQ + h * RD:C_RQ + (h + 1) * RD]
                    i = h * NT + t
                    nc.vector.tensor_scalar(v, v, mv[:, i, 0:1], rrs[:, i:i + 1], ALU.subtract, ALU.mult).then_inc(r_n, 1)
                if t >= 2:
                    lo_parts(ACT_EV["c"] + 2 * (t - 2), TURNED["c"] + 2 * (t - 2), t_hi, t_lo, (t - 2) * P)
            lo_parts(ACT_EV["c"] + 2 * (NT - 2), TURNED["c"] + 2 * (NT - 2), t_hi, t_lo, (NT - 2) * P)
            lo_parts(ACT_EV["c"] + 2 * (NT - 1), TURNED["c"] + 2 * (NT - 1), t_hi, t_lo, (NT - 1) * P)

            dve.wait_ge(gb_in, 48)
            for m in range(NM):
                invert(2 * NT + m)
                nc.vector.scalar_tensor_tensor(out=mem_t[:, m, :], in0=mem_t[:, m, :],
                                               scalar=rstd[:, 2 * NT + m:2 * NT + m + 1], in1=gain_b[:, :],
                                               op0=ALU.mult, op1=ALU.mult).then_inc(scaled, 1)

            def norm_steps(i0, items):
                for i in items:
                    kind, t = SEQ[i]
                    invert(i0 + i)
                    r = rstd[:, i0 + i:i0 + i + 1]
                    if kind == "post":
                        after_product(t, r)
                    else:
                        nc.vector.scalar_tensor_tensor(out=y[:, t, :], in0=x1[:, t, :], scalar=r, in1=gain_b[:, :],
                                                       op0=ALU.mult, op1=ALU.mult).then_inc(scaled, 1)

            def after_product(t, r):
                nc.vector.scalar_tensor_tensor(out=y[:, t, :], in0=y[:, t, :], scalar=r, in1=gain_a[:, :],
                                               op0=ALU.mult, op1=ALU.mult).then_inc(r_post, 1)

            def norm_stage(i0, stage):
                def lo(t):
                    base = H2_HI(t) if stage == "h2" else ACT_EV["h3"] + 2 * t
                    lo_parts(base, TURNED[stage] + 2 * t, t_hi, t_lo, t * P)

                n = len(SEQ)
                norm_steps(i0, range(n - 3))
                if stage == "h2":
                    for m in range(NM):
                        lo_parts(ACT_EV["mem"] + 2 * m, TURNED["mem"] + 2 * m, m_hi, m_lo, m * P)
                    norm_steps(i0, range(n - 3, n))
                    for t in range(NT):
                        lo(t)
                else:
                    norm_steps(i0, [n - 3])
                    lo(0)
                    norm_steps(i0, [n - 2])
                    lo(1)
                    lo(2)
                    norm_steps(i0, [n - 1])
                    for t in range(3, NT):
                        lo(t)

            dve.wait_ge(ga_in, 32)
            dve.wait_ge(gb_in, 64)
            norm_stage(I_H2, "h2")

            def mem_max(t):
                dve.wait_ge(x_sc, t + 1)
                b = 2 * (t % 2)
                nc.vector.tensor_reduce(wmx[:, t, 0:XH],
                                        ps[:, b:b + 2, :].rearrange("p b (h m) -> p (b h) m", h=2), AX.X,
                                        ALU.max).then_inc(x_mx, 1)
                dve.wait_ge(x_mx, 2 * t + 1)
                nc.vector.tensor_scalar(wnm[:, t, 0:XH], wmx[:, t, 0:XH], -X_SCALE, None, ALU.mult).then_inc(x_mx, 1)

            def normalise(t):
                dve.wait_ge(x_exp, XH * (t + 1))
                nc.vector.reciprocal(wrd[:, t, 0:XH], wrs[:, t, 0:XH]).then_inc(x_nrm, 1)
                dve.wait_ge(x_nrm, 2 * t + 1)
                nc.vector.tensor_tensor(px[:, t % 2, :, :], px[:, t % 2, :, :],
                                        wrd[:, t, 0:XH].unsqueeze(2).broadcast_to([P, XH, N_MEM]),
                                        ALU.mult).then_inc(x_nrm, 1)

            mem_max(0)
            for t in range(NT):
                if t != 4:
                    normalise(t)
                if t + 1 < NT:
                    mem_max(t + 1)
                dve.wait_ge(x_tr, 2 * t + 2)
                if t >= 4:
                    dve.wait_ge(x_pv, NK)
                nc.vector.tensor_copy(pTx[:, :, 2:4, (t % 4) * P:(t % 4 + 1) * P],
                                      bank(5).rearrange("p (h m i) -> p m h i", h=2, m=2)).then_inc(x_pd, 1)
                if t == 3:
                    normalise(4)
                if t % 4 == 3:
                    half = t // 4
                    for d in range(NK):
                        dve.wait_ge(x_hi, NK * half + d + 1)
                        c = slice(half * 512, (half + 1) * 512)
                        nc.vector.tensor_tensor(t_lo[:, d, c], bank(6 + d % 2), t_hi[:, d, c].bitcast(F32),
                                                ALU.subtract).then_inc(x_lo, 1)

            dve.wait_ge(ga_in, 48)
            dve.wait_ge(gb_in, 80)
            norm_stage(I_H3, "h3")

            def group(g, u):
                def prod(p):
                    dve.wait_ge(f_silu, g * 4 + (p + 1))
                    if p < 3:
                        dve.wait_ge(tile_done, g * 7 + (TILES["f"] + 2 * p + 2))
                    else:
                        dve.wait_ge(w_used, u + NK)
                    nc.vector.tensor_tensor(gs[:, p, :], gs[:, p, :], bank(2 * p + 1), ALU.mult).then_inc(dve_ev, 1)

                def low(p):
                    dve.wait_ge(f_high, g * 4 + (p + 1))
                    c = slice((p % 2) * 512, (p % 2 + 1) * 512)
                    nc.vector.tensor_tensor(f_lo[:, buf, p // 2, c], gs[:, p, :], f_hi[:, buf, p // 2, c].bitcast(F32),
                                            ALU.subtract).then_inc(f_low, 1)
                prod(0)
                prod(1)
                low(0)
                prod(2)
                low(1)
                prod(3)
                low(2)
                low(3)

            def accumulate(d, u, before):
                for c in range(2):
                    for t in range(NT):
                        if t < NT - 1:
                            dve.wait_ge(f_bank, d * 14 + (7 * c + t + 1))
                        else:
                            dve.wait_ge(w_used, u + (2 * c + 2))
                        if c == 0 and t == 0:
                            dve.wait_ge(dve_ev, before)
                        v = y[:, t, c * 512:(c + 1) * 512]
                        nc.vector.tensor_tensor(v, bank(t), v, ALU.add).then_inc(dve_ev, 1)

            buf = 0
            dve.wait_ge(y_zero, NT)
            group(0, U_F)
            with dve.Fori(0, NG // 2) as i:
                for odd in range(2):
                    buf = 1 - odd
                    u = i * 24 + (U_F + NK + 12 * odd)
                    group(i * 2 + (1 + odd), u)
                    accumulate(i * 2 + odd, u + NK, i * 40 + (F_EV + 20 * odd))
            last = F_EV + 20 * (NG - 1)
            dve.wait_ge(ga_in, 64)
            for t in range(NT + 2):
                if t < NT:
                    for c in range(2):
                        dve.wait_ge(f_bank, (NG - 1) * 14 + 2 * t + c + 1)
                        dve.wait_ge(dve_ev, last)
                        v = y[:, t, c * 512:(c + 1) * 512]
                        nc.vector.tensor_tensor(v, bank((2 * t + c) % 8), v, ALU.add).then_inc(dve_ev, 1)
                if t >= 2:
                    invert(I_END + t - 2)
                    dve.wait_ge(dve_ev, last + 2 * (t - 2) + 2)
                    after_product(t - 2, rstd[:, I_END + t - 2:I_END + t - 1])


_INS = ["x", "mem", "norm_mix_pre", "norm_mix_post", "w_in", "attn_sink", "attn_out_norm", "ret_decay_fwd",
        "ret_decay_bwd", "ret_gn", "w_out", "norm_xa_pre", "norm_xa_post", "norm_mem", "xa_wq", "xa_wkv", "xa_wo",
        "norm_ffn_pre", "norm_ffn_post", "ffn_w_gu", "ffn_w_down"]
_OUTS = [((1, S, D), "float32")]


def kernel(**inputs):
    import numpy as _np
    import concourse.bacc as _bacc
    from concourse import mybir as _mybir
    from concourse.bass_utils import run_bass_kernel_spmd as _run

    nc = _bacc.Bacc("TRN2", target_bir_lowering=False, num_devices=1)
    arrays, args = {}, []
    for name in _INS:
        arrays[f"in_{name}_dram"] = _np.ascontiguousarray(inputs[name])
    for name, a in host_constants().items():
        arrays[f"const_{name}_dram"] = a
    for name, a in arrays.items():
        args.append(nc.dram_tensor(name, a.shape, _mybir.dt.from_np(a.dtype), kind="ExternalInput").ap())
    for i, (shape, dtype) in enumerate(_OUTS):
        dt = _mybir.dt.from_np(_np.dtype(dtype))
        args.append(nc.dram_tensor(f"out_{i}_dram", shape, dt, kind="ExternalOutput").ap())
    build(nc, *args)
    r = _run(nc, [arrays], core_ids=[0])
    return r.results[0]["out_0_dram"]
```
